# Optimizing a Trainium2 kernel written in Bass

```python
import jax, jax.numpy as jnp
from jax import lax
import numpy as np

D_MODEL = 1024
BATCH = 1
SEQ = 256
DEPTH = 2
DEC_BATCH = 8
DEC_SEQ = 4
PAST_LEN = 2048
PAGE_SIZE = 128

N_META = 16
POOL_WINDOWS = (2, 4, 8, 16)
N_POOL_GROUPS = len(POOL_WINDOWS)
POOL_GROUP = D_MODEL // N_POOL_GROUPS
POOL_CTX = max(POOL_WINDOWS) - 1
CONV_WIDTH = 31
CONV_CTX = CONV_WIDTH - 1
D_FF = ((8 * D_MODEL // 3 + 255) // 256) * 256
N_EXPERTS = 8
TOP_K = 2
N_POOL_LAYERS = (DEPTH + 1) // 2
N_CONV_LAYERS = DEPTH // 2
DEEPNORM_ALPHA = float((2 * DEPTH) ** 0.25)
DEEPNORM_BETA = float((8 * DEPTH) ** -0.25)
LN_EPS = 1e-5

kernel_name = "hybrid_pool_conformer_deepnorm_moe_step"

def layer_norm(x, g, b):
    xf = x.astype(jnp.float32)
    mu = jnp.mean(xf, axis=-1, keepdims=True)
    xc = xf - mu
    var = jnp.mean(xc * xc, axis=-1, keepdims=True)
    y = xc * lax.rsqrt(var + LN_EPS) * g.astype(jnp.float32) + b.astype(jnp.float32)
    return y.astype(x.dtype)

def pool_mixer(x, prev, pos0, w, scale):
    T = x.shape[1]
    ext = jnp.concatenate([prev.astype(x.dtype), x], axis=1)
    cs = jnp.cumsum(ext.astype(jnp.float32), axis=1)
    cs0 = jnp.pad(cs, ((0, 0), (1, 0), (0, 0)))
    pos = pos0 + jnp.arange(T)
    xf = x.astype(jnp.float32)
    diffs = []
    for g, wg in enumerate(POOL_WINDOWS):
        lo, hi = g * POOL_GROUP, (g + 1) * POOL_GROUP
        s = cs0[:, POOL_CTX + 1:POOL_CTX + 1 + T, lo:hi] - cs0[:, POOL_CTX + 1 - wg:POOL_CTX + 1 - wg + T, lo:hi]
        cnt = jnp.minimum(pos + 1, wg).astype(jnp.float32)[None, :, None]
        diffs.append(s / cnt - xf[..., lo:hi])
    d = jnp.stack(diffs, axis=2)
    y = jnp.einsum('btgc,gce->btge', d, w.astype(jnp.float32)).reshape(x.shape)
    y = y * scale.astype(jnp.float32)
    return y.astype(x.dtype), ext[:, -POOL_CTX:]

def conv_module(x, prev, w1, b1, dw, dwb, lng, lnb, w2, b2):
    h = jnp.dot(x, w1) + b1
    a, gt = jnp.split(h, 2, axis=-1)
    u = a * jax.nn.sigmoid(gt)
    ext = jnp.concatenate([prev.astype(u.dtype), u], axis=1)
    c = lax.conv_general_dilated(ext, dw.astype(ext.dtype)[:, None, :], window_strides=(1,), padding='VALID',
                                 dimension_numbers=('NWC', 'WIO', 'NWC'), feature_group_count=D_MODEL)
    c = layer_norm(c + dwb, lng, lnb)
    y = jnp.dot(jax.nn.silu(c), w2) + b2
    return y.astype(x.dtype), ext[:, -CONV_CTX:]

def swiglu(x, wg, wu, wd):
    return jnp.dot(jax.nn.silu(jnp.dot(x, wg)) * jnp.dot(x, wu), wd)

def moe_swiglu(x, router, wg, wu, wd):
    shp = x.shape
    xf = x.reshape(-1, shp[-1])
    logits = jnp.dot(xf, router).astype(jnp.float32)
    top_v, top_i = lax.top_k(logits, TOP_K)
    probs = jax.nn.softmax(top_v, axis=-1)
    gate = jnp.sum(jax.nn.one_hot(top_i, N_EXPERTS, dtype=jnp.float32) * probs[..., None], axis=1)
    y = jnp.zeros(xf.shape, jnp.float32)
    for e in range(N_EXPERTS):
        y = y + gate[:, e:e + 1] * swiglu(xf, wg[e], wu[e], wd[e]).astype(jnp.float32)
    return y.astype(x.dtype).reshape(shp)

def trunk(x, pool_prev, conv_prev, pos0, pool_w, pool_scale, conv_w1, conv_b1, conv_dw, conv_dw_b,
          conv_ln_g, conv_ln_b, conv_w2, conv_b2, ln_mix_g, ln_mix_b, ln_ffn_g, ln_ffn_b,
          ffn_w_gate, ffn_w_up, ffn_w_down, moe_router, moe_w_gate, moe_w_up, moe_w_down):
    new_pool, new_conv = [], []
    for i in range(DEPTH):
        j = i // 2
        if i % 2 == 0:
            h, s = pool_mixer(x, pool_prev[j], pos0, pool_w[j], pool_scale[j])
            new_pool.append(s)
        else:
            h, s = conv_module(x, conv_prev[j], conv_w1[j], conv_b1[j], conv_dw[j], conv_dw_b[j],
                               conv_ln_g[j], conv_ln_b[j], conv_w2[j], conv_b2[j])
            new_conv.append(s)
        x = layer_norm(DEEPNORM_ALPHA * x + h, ln_mix_g[i], ln_mix_b[i])
        if i % 2 == 0:
            f = swiglu(x, ffn_w_gate[j], ffn_w_up[j], ffn_w_down[j]).astype(x.dtype)
        else:
            f = moe_swiglu(x, moe_router[j], moe_w_gate[j], moe_w_up[j], moe_w_down[j])
        x = layer_norm(DEEPNORM_ALPHA * x + f, ln_ffn_g[i], ln_ffn_b[i])
    return x, jnp.stack(new_pool), jnp.stack(new_conv)

def setup_inputs(seed: int = 0) -> dict:
    key = jax.random.key(seed)
    ks = jax.random.split(key, 32)
    n = lambda k, shape, s: jax.random.normal(k, shape, jnp.float32) * s
    D, F, E = D_MODEL, D_FF, N_EXPERTS
    NP, NC = N_POOL_LAYERS, N_CONV_LAYERS
    return {
        "x_prompt": n(ks[0], (BATCH, SEQ, D), 1.0),
        "x_sample": n(ks[1], (DEC_BATCH, DEC_SEQ, D), 1.0),
        "state_pool": n(ks[2], (NP, DEC_BATCH, POOL_CTX, D), 1.0),
        "state_conv": n(ks[3], (NC, DEC_BATCH, CONV_CTX, D), 0.5),
        "meta": n(ks[4], (N_META, D), 1.0),
        "pool_w": n(ks[5], (NP, N_POOL_GROUPS, POOL_GROUP, POOL_GROUP), DEEPNORM_BETA * POOL_GROUP ** -0.5),
        "pool_scale": 1.0 + n(ks[6], (NP, D), 0.1),
        "conv_w1": n(ks[7], (NC, D, 2 * D), D ** -0.5),
        "conv_b1": n(ks[8], (NC, 2 * D), 0.02),
        "conv_dw": n(ks[9], (NC, CONV_WIDTH, D), CONV_WIDTH ** -0.5),
        "conv_dw_b": n(ks[10], (NC, D), 0.02),
        "conv_ln_g": 1.0 + n(ks[11], (NC, D), 0.05),
        "conv_ln_b": n(ks[12], (NC, D), 0.02),
        "conv_w2": n(ks[13], (NC, D, D), DEEPNORM_BETA * D ** -0.5),
        "conv_b2": n(ks[14], (NC, D), 0.02),
        "ln_mix_g": 1.0 + n(ks[15], (DEPTH, D), 0.05),
        "ln_mix_b": n(ks[16], (DEPTH, D), 0.02),
        "ln_ffn_g": 1.0 + n(ks[17], (DEPTH, D), 0.05),
        "ln_ffn_b": n(ks[18], (DEPTH, D), 0.02),
        "ffn_w_gate": n(ks[19], (NP, D, F), D ** -0.5),
        "ffn_w_up": n(ks[20], (NP, D, F), D ** -0.5),
        "ffn_w_down": n(ks[21], (NP, F, D), DEEPNORM_BETA * F ** -0.5),
        "moe_router": n(ks[22], (NC, D, E), D ** -0.5),
        "moe_w_gate": n(ks[23], (NC, E, D, F), D ** -0.5),
        "moe_w_up": n(ks[24], (NC, E, D, F), D ** -0.5),
        "moe_w_down": n(ks[25], (NC, E, F, D), DEEPNORM_BETA * F ** -0.5),
    }

def reference(x_prompt, x_sample, state_pool, state_conv, meta, pool_w, pool_scale, conv_w1, conv_b1,
              conv_dw, conv_dw_b, conv_ln_g, conv_ln_b, conv_w2, conv_b2, ln_mix_g, ln_mix_b,
              ln_ffn_g, ln_ffn_b, ffn_w_gate, ffn_w_up, ffn_w_down, moe_router, moe_w_gate,
              moe_w_up, moe_w_down):
    weights = (pool_w, pool_scale, conv_w1, conv_b1, conv_dw, conv_dw_b, conv_ln_g, conv_ln_b,
               conv_w2, conv_b2, ln_mix_g, ln_mix_b, ln_ffn_g, ln_ffn_b, ffn_w_gate, ffn_w_up,
               ffn_w_down, moe_router, moe_w_gate, moe_w_up, moe_w_down)
    B = x_prompt.shape[0]
    meta_b = jnp.broadcast_to(meta.astype(x_prompt.dtype)[None], (B, N_META, D_MODEL))
    xp = jnp.concatenate([meta_b, x_prompt], axis=1)
    zero_pool = jnp.zeros((N_POOL_LAYERS, B, POOL_CTX, D_MODEL), x_prompt.dtype)
    zero_conv = jnp.zeros((N_CONV_LAYERS, B, CONV_CTX, D_MODEL), x_prompt.dtype)
    yp, pool_p, conv_p = trunk(xp, zero_pool, zero_conv, 0, *weights)
    ys, pool_s, conv_s = trunk(x_sample, state_pool, state_conv, PAST_LEN, *weights)
    y_prompt = yp[:, N_META:]
    return (y_prompt, ys, pool_p, conv_p, pool_s, conv_s)


_drawn_inputs = setup_inputs


def setup_inputs(seed=0):
    import zlib

    import numpy as np

    out = dict(_drawn_inputs(seed))
    spreads = {}
    factors = {'conv_b1': 2.691,
     'conv_dw_b': 3.008,
     'conv_ln_g': 2.682,
     'conv_ln_b': 10.099,
     'conv_b2': 4.054}
    for name, (base, spread) in spreads.items():
        noise = np.random.default_rng([zlib.crc32(name.encode()), seed]).standard_normal(out[name].shape)
        drawn = base * np.exp(spread * noise) if base else spread * noise
        out[name] = __import__('jax').numpy.asarray(drawn.astype(out[name].dtype))
    for name, factor in factors.items():
        out[name] = (out[name] * factor).astype(out[name].dtype)
    return out
```

```python
from contextlib import ExitStack

import concourse.bass as bass
from concourse import mybir

F32 = mybir.dt.float32
F32R = mybir.dt.float32r
I32 = mybir.dt.int32
U32 = mybir.dt.uint32
ALU = mybir.AluOpType
ACT = mybir.ActivationFunctionType
AX = mybir.AxisListType

P = 128
RAW = 11
SPLIT = 3
LN_EPS = 1e-5
WINDOWS = (2, 4, 8, 16)
NEG = -1.0


def build_trunk(nc, x_prompt, x_sample, state_pool, state_conv, meta, pool_w, pool_scale, conv_w1,
                conv_b1, conv_dw, conv_dw_b, conv_ln_g, conv_ln_b, conv_w2, conv_b2, ln_mix_g,
                ln_mix_b, ln_ffn_g, ln_ffn_b, ffn_w_gate, ffn_w_up, ffn_w_down, moe_router,
                moe_w_gate, moe_w_up, moe_w_down, y_prompt, y_sample, new_pool_prompt,
                new_conv_prompt, new_pool_sample, new_conv_sample):
    D = x_prompt.shape[2]
    KC = D // P
    SEQ = x_prompt.shape[1]
    SB, ST_ = x_sample.shape[:2]
    META = meta.shape[0]
    PCTX = state_pool.shape[2]
    CCTX = state_conv.shape[2]
    TAPS = conv_dw.shape[1]
    F = ffn_w_gate.shape[2]
    E = moe_router.shape[2]
    NPR = META + SEQ
    NS = SB * ST_
    NT = NPR + NS
    NM = SEQ + NS
    ALPHA = float(4) ** 0.25
    HALF = D // 2
    TW = 256
    TR = 2
    NJ = F // TW
    FC = F // P
    IN_ROWS = (P, P, NT - 2 * P)
    OUT_ROWS = (P, P, NM - 2 * P)
    T_DOWN = 2 * NJ
    T_W1 = 3 * NJ
    NW1 = 2 * D // TW
    T_W2 = T_W1 + NW1
    NW2 = D // TW
    T_MOE = T_W2 + NW2
    TE = 3 * NJ
    assert TE % RAW == 0 and TE % SPLIT == 0

    with ExitStack() as ctx:
        ring_at = 16512
        split_at = ring_at + RAW * 8192
        const_at = split_at + 2 * SPLIT * 8192
        place = [const_at]

        def at(name, shape, dt, offset):
            assert offset % 32 == 0, (name, offset)
            return nc.alloc_sbuf_tensor_at(name, shape, dt, offset=offset)

        def const(name, shape, dt=F32):
            n = 4
            for s in shape[1:]:
                n *= s
            t = at(name, shape, dt, place[0])
            place[0] += (n + 31) // 32 * 32
            return t

        raw = [at(f"raw{i}", [P, 2048], F32, ring_at + 8192 * i) for i in range(RAW)]
        w_hi = [at(f"w_hi{i}", [P, 2048], F32R, split_at + 16384 * i) for i in range(SPLIT)]
        w_lo = [at(f"w_lo{i}", [P, 2048], F32R, split_at + 16384 * i + 8192) for i in range(SPLIT)]

        ident = const("ident", [P, P])
        mean_mat = const("mean_mat", [P, P])
        ones = const("ones", [P, P])
        before = const("before", [P, P])
        slot_no = const("slot_no", [P, P])
        vec = const("vec", [P, 104 + KC * TAPS])
        eps = const("eps", [P, 1])
        router = const("router", [P, KC, E])
        logits = const("logits", [P, 3, E])
        top_v = const("top_v", [P, 3, 8])
        top_i = const("top_i", [P, 3, 8], U32)
        top_f = const("top_f", [P, 3, 2])
        prob = const("prob", [P, 3, 4])
        pick1 = const("pick1", [P, 3, E])
        pick2 = const("pick2", [P, 3, E])
        taken = const("taken", [P, 3, E])
        gate = const("gate", [P, 3, 1 + E])
        slot_of = const("slot_of", [P, 3, E + 1])
        most = const("most", [P, 1])
        most_i = const("most_i", [P, 1], I32)
        mv = const("mv", [P, 3, 2])
        std3 = const("std3", [P, 3])
        shift3 = const("shift3", [P, 3])
        work = place[0]
        end = 229368

        def area(name, shape, dt, offset):
            n = 4
            for s in shape[1:]:
                n *= s
            assert work + offset + n <= end, (name, work + offset + n - end)
            return at(name, shape, dt, work + offset)

        XB = KC * NT * 4
        zT = area("zT", [P, KC, NT], F32, 0)
        x_hi = area("x_hi", [P, KC, NT], F32R, XB)
        x_lo = area("x_lo", [P, KC, NT], F32R, 2 * XB)
        A3 = 3 * XB
        PEXT = PCTX + NPR + SB * (PCTX + ST_)
        pext = area("pext", [P, KC, PEXT], F32, A3)
        dT = area("dT", [P, KC, NT], F32, A3 + KC * PEXT * 4)
        sq = area("sq", [P, KC, NT], F32, A3)
        FIRST_BORROWED = 6
        slot = lambda i: ring_at + 8192 * i
        win_a = at("win_a", [P, 2, PEXT], F32, slot(6))
        win_b = at("win_b", [P, 2, PEXT], F32, slot(6) + 3520)
        recip = at("recip", [P, 16], F32, slot(6) + 7168)
        xin = at("xin", [P, 3, D], F32, slot(7))
        spool = at("spool", [P, D], F32, slot(8) + 4096)
        poolw = at("poolw", [P, 4, 2, 256], F32, slot(9))
        vrows = at("vrows", [P, 3, P], F32, slot(10))
        h = area("h", [P, FC, NT], F32, A3)
        JB = A3 + FC * NT * 4
        h_hi = [area(f"h_hi{i}", [P, 2, NT], F32R, JB + 4864 * i) for i in range(2)]
        h_lo = [area(f"h_lo{i}", [P, 2, NT], F32R, JB + 4864 * i + 2432) for i in range(2)]
        sg = [area(f"sg{i}", [P, NT], F32, JB + 9728 + 1216 * i) for i in range(2)]
        rs = sg[0]
        UP = CCTX + NPR
        UEXT = UP + SB * (CCTX + ST_)
        uext = area("uext", [P, KC, UEXT], F32, A3)
        A4 = A3 + KC * UEXT * 4
        sconv = area("sconv", [P, 2, D], F32, A4)
        unat = area("unat", [32, 2, D], F32, A4)
        cacc = area("cacc", [P, KC, NM], F32, A4 + 8192)
        M0 = XB
        xn_hi = area("xn_hi", [P, 3, D], F32R, M0)
        xn_lo = area("xn_lo", [P, 3, D], F32R, M0 + 12288)
        acc = area("acc", [P, 3, D], F32, M0 + 24576)
        M1 = M0 + 36864
        xg_hi = area("xg_hi", [P, KC, P], F32R, M1)
        xg_lo = area("xg_lo", [P, KC, P], F32R, M1 + 4096)
        hn = area("hn", [P, TW], F32, M1 + 8192)
        stats = area("stats", [P, 3, 2, 6], F32, M1 + 8192)
        sgn = area("sgn", [P, TW], F32, M1 + 9216)
        ht_hi = area("ht_hi", [P, TR, P], F32R, M1 + 10240)
        ht_lo = area("ht_lo", [P, TR, P], F32R, M1 + 11264)
        sel_t = area("sel_t", [P, NM], F32R, M1 + 12288)
        g_row = area("g_row", [P, D], F32, M1 + 13440)
        b_row = area("b_row", [P, D], F32, M1 + 17536)
        yy_hi = area("yy_hi", [P, D], F32R, 0)
        yy_lo = area("yy_lo", [P, D], F32R, 4096)
        sel = area("sel", [P, 3, P], F32R, 8192)

        ps = [ctx.enter_context(nc.psum_tensor(f"bank{i}", [P, 512], F32)) for i in range(8)]

        def sem(name):
            return ctx.enter_context(nc.semaphore(name))

        raw_landed = [sem(f"raw_landed{i}") for i in range(RAW)]
        x_landed = [sem(f"x_landed{i}") for i in range(3)]
        spool_landed = sem("spool_landed")
        poolw_landed = sem("poolw_landed")
        vec_landed = sem("vec_landed")
        router_landed = sem("router_landed")
        sconv_landed = sem("sconv_landed")
        rows_landed = sem("rows_landed")
        stored = sem("stored")
        u_stored = sem("u_stored")
        hi_ready = sem("hi_ready")
        split_ready = sem("split_ready")
        tile_used = sem("tile_used")
        consts_ready = sem("consts_ready")
        ctx_zeroed = sem("ctx_zeroed")
        turned = sem("turned")
        evac_v = sem("evac_v")
        evac_a = sem("evac_a")
        dve_step = sem("dve_step")
        act_step = sem("act_step")
        pool_step = sem("pool_step")
        d_ready = sem("d_ready")
        resid_ready = sem("resid_ready")
        scaled = sem("scaled")
        pooled = sem("pooled")
        z_done = sem("z_done")
        mean_done = sem("mean_done")
        xc_done = sem("xc_done")
        sq_done = sem("sq_done")
        var_done = sem("var_done")
        std_done = sem("std_done")
        yg_done = sem("yg_done")
        y_done = sem("y_done")
        act_of_y = sem("act_of_y")
        xhi_done = sem("xhi_done")
        xlo_done = sem("xlo_done")
        silu_done = sem("silu_done")
        h_done = sem("h_done")
        jhi_done = sem("jhi_done")
        jlo_done = sem("jlo_done")
        down_done = sem("down_done")
        sig_done = sem("sig_done")
        u_done = sem("u_done")
        conv_step = sem("conv_step")
        routed = sem("routed")
        gap_ready = sem("gap_ready")
        exp_done = sem("exp_done")
        slots_moved = sem("slots_moved")
        mask_ready = sem("mask_ready")
        placed = sem("placed")
        flag_ready = sem("flag_ready")
        acc_ready = sem("acc_ready")
        sel_ready = sem("sel_ready")
        gathered = sem("gathered")
        xg_hi_done = sem("xg_hi_done")
        xg_lo_done = sem("xg_lo_done")
        h_turned = sem("h_turned")
        ht_hi_done = sem("ht_hi_done")
        ht_lo_done = sem("ht_lo_done")
        sel_turned = sem("sel_turned")
        sel_t_done = sem("sel_t_done")
        yy_hi_done = sem("yy_hi_done")
        yy_lo_done = sem("yy_lo_done")
        spread = sem("spread")
        summed = sem("summed")
        fin_stats = sem("fin_stats")
        fin_std = sem("fin_std")
        fin_recip = sem("fin_recip")
        fin_norm = sem("fin_norm")
        fin_g = sem("fin_g")
        fin_out = sem("fin_out")

        V_SCALE, V_B1, V_DWB, V_CG, V_CB, V_B2, V_MG, V_MB, V_FG, V_FB, V_DW = (
            0, 8, 24, 32, 40, 48, 56, 72, 88, 96, 104)

        def v(col):
            return vec[:, col:col + 1]

        def wide(t):
            return t[:, :].rearrange("p (k f) -> p k f", k=KC)

        def tall(t):
            return t[:, :].rearrange("p (k f) -> p k f", k=TR)

        pext_s = pext[:, :, PCTX + NPR:PEXT].rearrange("p c (b j) -> p c b j", b=SB)
        uext_s = uext[:, :, UP:UEXT].rearrange("p c (j b) -> p c b j", b=SB)

        norms = [
            (lambda c: zT[:, c, :], NT, V_MG, V_MB),
            (lambda c: zT[:, c, :], NT, V_FG, V_FB),
            (lambda c: cacc[:, c, :], NM, V_CG, V_CB),
            (lambda c: zT[:, c, META:NT], NM, V_MG + KC, V_MB + KC),
        ]

        IN_JOBS = [(i, half) for i in range(3) for half in range(2)] + [("pool", 0), ("pool", 1), ("vec", 0)]
        VEC_JOB = len(IN_JOBS) - 1
        N_IN = len(IN_JOBS)
        CONV_JOBS = [(i, half) for i in range(2) for half in range(2)]
        U_JOBS = [(part, half) for part in range(2) for half in range(2)]
        X_JOBS = [(i, half) for i in range(3) for half in range(2)]
        T_CONVJ = N_IN
        T_UJ = T_CONVJ + len(CONV_JOBS)
        T_XJ = T_UJ + len(U_JOBS)
        A_IN = 5
        A_CONV = A_IN + len(CONV_JOBS)
        A_U = A_CONV + len(U_JOBS)
        RTOT = E + 1
        SCAT = 6 * (E + 1)

        block = ctx.enter_context(nc.Block())

        @block.sync
        def _(sp):
            def load(t, src, dst):
                if t >= RAW:
                    sp.wait_ge(split_ready, t - RAW + 1)
                elif t == FIRST_BORROWED:
                    sp.wait_ge(z_done, KC)
                sp.dma_start(dst(raw[t % RAW]), src).then_inc(raw_landed[t % RAW], 16)

            sp.dma_start(xin[META:P, 0, :], x_prompt[0, 0:P - META, :]).then_inc(x_landed[0], 16)
            sp.dma_start(xin[:, 1, :], x_prompt[0, P - META:2 * P - META, :]).then_inc(x_landed[1], 16)
            sp.dma_start(xin[META:META + NS, 2, :], x_sample.rearrange("b t d -> (b t) d")).then_inc(x_landed[2], 16)
            sp.dma_start(poolw[:], pool_w[0].rearrange("g (c p) e -> p g c e", p=P)).then_inc(poolw_landed, 16)
            for i in range(NJ):
                for k, w in ((0, ffn_w_gate), (1, ffn_w_up)):
                    load(2 * i + k, w[0, :, i * TW:(i + 1) * TW].rearrange("(c p) f -> p c f", p=P), wide)
            for i in range(NJ):
                load(T_DOWN + i, ffn_w_down[0, i * TW:(i + 1) * TW, :].rearrange("(c p) f -> p c f", p=P), tall)
            for i in range(NW1 // 2):
                for k in range(2):
                    lo = k * D + i * TW
                    load(T_W1 + 2 * i + k, conv_w1[0, :, lo:lo + TW].rearrange("(c p) f -> p c f", p=P), wide)
            sp.wait_ge(jlo_done, NJ)
            for i in range(2):
                sp.dma_start(sconv[0:4 * CCTX, i, :],
                             state_conv[0, 4 * i:4 * i + 4].rearrange("b j d -> (b j) d")).then_inc(sconv_landed, 16)
            for i in range(NW2):
                load(T_W2 + i, conv_w2[0, :, i * TW:(i + 1) * TW].rearrange("(c p) f -> p c f", p=P), wide)

            def expert_tile(e, j):
                if j < 2:
                    kind, i = j, 0
                elif j == TE - 1:
                    kind, i = 2, NJ - 1
                else:
                    kind, i = (j + 1) % 3, (j + 1) // 3
                    i -= kind == 2
                if kind == 2:
                    src = moe_w_down[0].rearrange("e (j r) f -> (e j) r f", r=TW)[bass.ds(e * NJ + i, 1)]
                    return src.rearrange("o (c p) f -> p (o c) f", p=P), tall
                w = (moe_w_gate, moe_w_up)[kind]
                return w[0, bass.ds(e, 1), :, i * TW:(i + 1) * TW].rearrange("o (c p) f -> p (o c) f", p=P), wide

            def load_expert(n, e, j):
                t = T_MOE + j
                sp.wait_ge(split_ready, n * TE + (t - RAW + 1))
                src, dst = expert_tile(e, j) if j < TE else expert_tile((e + 1) % E, j - TE)
                sp.dma_start(dst(raw[t % RAW]), src).then_inc(raw_landed[t % RAW], 16)

            for j in range(2):
                load_expert(0, 0, j)
            sp.dma_start(new_pool_prompt[0, 0], x_prompt[0, SEQ - PCTX:SEQ, :]).then_inc(stored, 16)
            sp.dma_start(new_pool_sample[0, :, 0:PCTX - ST_, :], state_pool[0, :, ST_:PCTX, :]).then_inc(stored, 16)
            sp.dma_start(new_pool_sample[0, :, PCTX - ST_:PCTX, :], x_sample).then_inc(stored, 16)
            sp.dma_start(new_conv_sample[0, :, 0:CCTX - ST_, :], state_conv[0, :, ST_:CCTX, :]).then_inc(stored, 16)
            sp.wait_ge(evac_a, A_U)
            sp.dma_start(new_conv_prompt[0, 0], unat[0:CCTX, 0, :]).then_inc(u_stored, 16)
            for t in range(ST_):
                sp.dma_start(new_conv_sample[0, :, CCTX - ST_ + t, :],
                             unat[t * SB:(t + 1) * SB, 1, :]).then_inc(u_stored, 16)

            def one_pass(r):
                with sp.Fori(0, E) as e:
                    for j in range(2, TE + 2):
                        load_expert(r * E + e, e, j)

            one_pass(0)
            sp.wait_ge(acc_ready, 6)
            sp.dma_start(g_row[:], ln_ffn_g[1, :].partition_broadcast(P)).then_inc(rows_landed, 16)
            sp.dma_start(b_row[:], ln_ffn_b[1, :].partition_broadcast(P)).then_inc(rows_landed, 16)
            sp.wait_ge(flag_ready, 1)
            largest = sp.value_load(most_i[0:1, 0:1], min_val=0, max_val=NM)
            with sp.If(largest > P):
                with sp.Fori(1, 3) as r:
                    one_pass(r)
                for j in range(2):
                    t = T_MOE + 3 * E * TE + j
                    sp.wait_ge(raw_landed[t % RAW], 16 * (t // RAW + 1))
            for j in range(2):
                t = T_MOE + E * TE + j
                sp.wait_ge(raw_landed[t % RAW], 16 * (t // RAW + 1))
            for i in range(3):
                sp.wait_ge(fin_out, i + 1)
                if i < 2:
                    sp.dma_start(y_prompt[0, i * P:(i + 1) * P, :], acc[:, i, :]).then_inc(stored, 16)
                else:
                    sp.dma_start(y_sample.rearrange("b t d -> (b t) d"), acc[0:NS, i, :]).then_inc(stored, 16)
            sp.wait_ge(u_stored, 16 * (1 + ST_))
            sp.wait_ge(stored, 16 * (4 + 3))

        @block.gpsimd
        def _(pool):
            pool.memset(ident[:], 0.0).then_inc(pool_step, 1)
            pool.wait_ge(pool_step, 1)
            pool.affine_select(out=ident[:], in_=ident[:], compare_op=ALU.not_equal, fill=1.0, base=0,
                               pattern=[[-1, P]], channel_multiplier=1).then_inc(consts_ready, 1)
            pool.memset(mean_mat[:], 1.0 / D).then_inc(consts_ready, 1)
            pool.memset(pext[:, :, 0:PCTX], 0.0).then_inc(ctx_zeroed, 1)
            pool.memset(eps[:], LN_EPS).then_inc(consts_ready, 1)
            pool.iota(slot_no[:], pattern=[[1, P]], base=0, channel_multiplier=0,
                      allow_small_or_imprecise_dtypes=True).then_inc(consts_ready, 1)
            pool.memset(ones[:], 1.0).then_inc(consts_ready, 1)
            pool.memset(before[:], 1.0).then_inc(pool_step, 1)
            pool.wait_ge(pool_step, 2)
            pool.affine_select(out=before[:], in_=before[:], compare_op=ALU.is_ge, fill=0.0, base=-1,
                               pattern=[[1, P]], channel_multiplier=-1).then_inc(consts_ready, 1)
            for t in (logits, gate, taken, slot_of):
                pool.memset(t[:], 0.0 if t is not slot_of else NEG).then_inc(consts_ready, 1)
            pool.wait_ge(var_done, 2)
            pool.memset(uext[:, :, 0:CCTX], 0.0).then_inc(ctx_zeroed, 1)
            pool.wait_ge(var_done, 4)
            pool.memset(xn_hi[:, 2, :].bitcast(F32), 0.0).then_inc(ctx_zeroed, 1)
            pool.memset(xn_lo[:, 2, :].bitcast(F32), 0.0).then_inc(ctx_zeroed, 1)
        N_CONSTS = 10

        @block.scalar
        def _(act):
            act.dma_start(xin[0:META, 0, :], meta).then_inc(x_landed[0], 16)
            act.dma_start(xin[0:META, 2, :], x_prompt[0, 2 * P - META:SEQ, :]).then_inc(x_landed[2], 16)
            act.dma_start(spool[0:SB * PCTX, :], state_pool[0].rearrange("b j d -> (b j) d")).then_inc(spool_landed, 16)
            rows = [(pool_scale[0:1], 1), (conv_b1[0:1], 2), (conv_dw_b[0:1], 1), (conv_ln_g[0:1], 1),
                    (conv_ln_b[0:1], 1), (conv_b2[0:1], 1), (ln_mix_g, 2), (ln_mix_b, 2),
                    (ln_ffn_g[0:1], 1), (ln_ffn_b[0:1], 1)]
            r0 = 0
            for src, k in rows:
                act.dma_start(vrows[r0:r0 + KC * k, 0, :],
                              src.rearrange("a (c p) -> (a c) p", p=P)).then_inc(vec_landed, 16)
                r0 += KC * k
            dw_rows = conv_dw[0].rearrange("k (c p) -> (k c) p", p=P)
            for i in range(2):
                act.dma_start(vrows[0:124, 1 + i, :], dw_rows[124 * i:124 * i + 124, :]).then_inc(vec_landed, 16)
            act.dma_start(router[:], moe_router[0].rearrange("(c p) e -> p c e", p=P)).then_inc(router_landed, 16)

            def hi(t, n=None):
                if n is None:
                    act.wait_ge(raw_landed[t % RAW], 16 * (t // RAW + 1))
                    if t >= SPLIT:
                        act.wait_ge(tile_used, t - SPLIT + 1)
                else:
                    act.wait_ge(raw_landed[t % RAW], n * (16 * TE // RAW) + 16 * (t // RAW + 1))
                    act.wait_ge(tile_used, n * TE + (t - SPLIT + 1))
                act.copy(w_hi[t % SPLIT][:], raw[t % RAW][:]).then_inc(hi_ready, 1)

            n_evac = 0
            for job, (i, half) in enumerate(IN_JOBS):
                c0 = half * 4
                src = ps[job % 8][:, :].rearrange("p (c n) -> p c n", c=4)
                if i == "pool":
                    act.wait_ge(turned, job + 1)
                    for c in range(4):
                        last = act.copy(pext_s[:, c0 + c, :, 0:PCTX],
                                        src[:, c, 0:SB * PCTX].rearrange("p (b j) -> p b j", b=SB))
                    last.then_inc(evac_a, 1)
                elif half == 1 and i in (0, 1):
                    act.wait_ge(turned, job + 1)
                    act.copy(pext[:, c0:c0 + 4, PCTX + P * i:PCTX + P * (i + 1)], src).then_inc(evac_a, 1)
                elif half == 1 and i == 2:
                    act.wait_ge(turned, job + 1)
                    act.copy(pext[:, c0:c0 + 4, PCTX + 2 * P:PCTX + NPR], src[:, :, 0:META])
                    for c in range(4):
                        last = act.copy(pext_s[:, c0 + c, :, PCTX:PCTX + ST_],
                                        src[:, c, META:META + NS].rearrange("p (b j) -> p b j", b=SB))
                    last.then_inc(evac_a, 1)
            act.wait_ge(evac_a, A_IN)
            act.wait_ge(evac_v, 3)
            act.mul(zT[:, :, 0:NPR], pext[:, :, PCTX:PCTX + NPR], ALPHA)
            for c in range(KC):
                last = act.mul(zT[:, c, NPR:NT].rearrange("p (b j) -> p b j", b=SB),
                               pext_s[:, c, :, PCTX:PCTX + ST_], ALPHA)
            last.then_inc(resid_ready, 1)
            hi(0)
            hi(1)

            def norm(L):
                z, n, g, b = norms[L]
                for c in range(KC):
                    act.wait_ge(xc_done, KC * L + c + 1)
                    act.activation(sq[:, c, 0:n], z(c), ACT.Square).then_inc(sq_done, 1)
                act.wait_ge(var_done, L + 1)
                act.activation(rs[:, 0:n], ps[1][:, 0:n], ACT.Sqrt, bias=eps[:, 0:1]).then_inc(std_done, 1)

            def split_x(L):
                z, n, g, b = norms[L]
                for c in range(KC):
                    act.wait_ge(y_done, KC * L + c + 1)
                    if L == 2:
                        act.activation(z(c), z(c), ACT.Silu).then_inc(act_of_y, 1)
                        act.wait_ge(act_of_y, c + 1)
                    act.copy(x_hi[:, c, 0:n], z(c)).then_inc(xhi_done, 1)

            def scale_residual(L, bias):
                for c in range(KC):
                    act.wait_ge(xlo_done, KC * L + c + 1)
                    if bias is None:
                        act.mul(zT[:, c, :], zT[:, c, :], ALPHA).then_inc(scaled, 1)
                    else:
                        act.activation(zT[:, c, :], zT[:, c, :], ACT.Identity, scale=ALPHA,
                                       bias=v(bias + c)).then_inc(scaled, 1)

            norm(0)
            split_x(0)
            scale_residual(0, None)
            for i in range(NJ):
                hi(2 * i + 2)
                hi(2 * i + 3)
                act.wait_ge(tile_used, 2 * i + 1)
                for s in range(2):
                    q = 2 * i + s
                    if q >= 2:
                        act.wait_ge(h_done, q - 1)
                    act.activation(sg[s][:], ps[2 * (q % 4)][:, 0:NT], ACT.Silu).then_inc(silu_done, 1)
            for i in range(-1, NJ):
                if i >= 0:
                    hi(T_DOWN + i + 2)
                if i + 1 < NJ:
                    act.wait_ge(h_done, 2 * (i + 2))
                    if i >= 1:
                        act.wait_ge(tile_used, T_DOWN + i)
                    act.copy(h_hi[(i + 1) % 2][:], h[:, 2 * i + 2:2 * i + 4, :]).then_inc(jhi_done, 1)
            norm(1)
            for k, (i, half) in enumerate(CONV_JOBS):
                act.wait_ge(turned, T_CONVJ + k + 1)
                src = ps[2 + k][:, :].rearrange("p (c n) -> p c n", c=4)
                for c in range(4):
                    last = act.copy(uext_s[:, 4 * half + c, 4 * i:4 * i + 4, 0:CCTX],
                                    src[:, c, 0:4 * CCTX].rearrange("p (b j) -> p b j", b=4))
                last.then_inc(evac_a, 1)
            split_x(1)
            scale_residual(1, V_B2)
            for i in range(NW1 // 2):
                hi(T_W1 + 2 * i + 2)
                hi(T_W1 + 2 * i + 3)
                act.wait_ge(tile_used, T_W1 + 2 * i + 2)
                for s in range(2):
                    q = 2 * i + s
                    if q >= 2:
                        act.wait_ge(u_done, q - 1)
                    act.activation(sg[s][:], ps[2 * (q % 4) + 1][:, 0:NT], ACT.Sigmoid,
                                   bias=v(V_B1 + KC + q)).then_inc(sig_done, 1)
            for k, (part, half) in enumerate(U_JOBS):
                act.wait_ge(turned, T_UJ + k + 1)
                n = (CCTX, NS)[part]
                act.copy(unat[0:n, part, half * HALF:(half + 1) * HALF], ps[2 + k][0:n, :]).then_inc(evac_a, 1)
            norm(2)
            split_x(2)
            for i in range(NW2):
                hi(T_W2 + 2 + i)
            norm(3)
            for k, (i, half) in enumerate(X_JOBS):
                n = OUT_ROWS[i]
                act.wait_ge(turned, T_XJ + k + 1)
                if i == 2:
                    act.wait_ge(ctx_zeroed, 4)
                cols = slice(half * HALF, (half + 1) * HALF)
                act.copy(xn_hi[0:n, i, cols], ps[(3 + k) % 8][0:n, :]).then_inc(xhi_done, 1)
                act.mul(acc[0:n, i, cols], ps[(3 + k) % 8][0:n, :], ALPHA).then_inc(acc_ready, 1)
            act.wait_ge(gap_ready, 1)
            act.activation(prob[:, :, 1:2], prob[:, :, 0:1], ACT.Exp).then_inc(exp_done, 1)
            act.wait_ge(u_stored, 16 * (1 + ST_))

            def xg_evac(g):
                for k in range(2):
                    act.wait_ge(gathered, 2 * g + (k + 1))
                    act.copy(xg_hi[:, 4 * k:4 * k + 4, :],
                             ps[1 + 2 * k][:, :].rearrange("p (c n) -> p c n", c=4)).then_inc(xg_hi_done, 1)

            def one_pass(r):
                xg_evac(r * RTOT)
                with act.Fori(0, E) as e:
                    n = r * E + e
                    t0 = n * TE

                    def silu(j, gate_tile):
                        act.wait_ge(tile_used, t0 + (T_MOE + gate_tile + 1))
                        act.wait_ge(h_done, n * NJ + (FC + j))
                        act.activation(sgn[:], ps[j % 2][:, 0:TW], ACT.Silu).then_inc(silu_done, 1)

                    def turn_evac(j):
                        act.wait_ge(h_turned, n * NJ + (j + 1))
                        act.copy(ht_hi[:], ps[4 + j % 2][:, 0:TR * P].rearrange("p (c n) -> p c n", c=TR))\
                            .then_inc(ht_hi_done, 1)

                    hi(T_MOE + 2, n)
                    hi(T_MOE + 3, n)
                    silu(0, 0)
                    for j in range(1, NJ):
                        g = 3 * j - 1
                        hi(T_MOE + g + 2, n)
                        turn_evac(j - 1)
                        if j == 1:
                            act.wait_ge(sel_turned, n + 1)
                            act.copy(sel_t[:], ps[5][:, 0:NM]).then_inc(sel_t_done, 1)
                        hi(T_MOE + g + 3, n)
                        silu(j, g)
                        hi(T_MOE + g + 4, n)
                    turn_evac(NJ - 1)
                    xg_evac(r * RTOT + e + 1)
                    hi(T_MOE + TE + 1, n)
                    act.wait_ge(tile_used, t0 + (T_MOE + TE))
                    for k in range(2):
                        act.copy(yy_hi[:, k * HALF:(k + 1) * HALF], ps[6 + k][:, :]).then_inc(yy_hi_done, 1)

            one_pass(0)
            act.wait_ge(flag_ready, 1)
            largest = act.value_load(most_i[0:1, 0:1], min_val=0, max_val=NM)
            with act.If(largest > P):
                with act.Fori(1, 3) as r:
                    one_pass(r)
            for i in range(3):
                n = OUT_ROWS[i]
                act.wait_ge(fin_stats, i + 1)
                act.activation(std3[0:n, i:i + 1], mv[0:n, i, 1:2], ACT.Sqrt, bias=eps[0:n, 0:1]).then_inc(fin_std, 1)
            for i in range(3):
                n = OUT_ROWS[i]
                act.wait_ge(fin_recip, i + 1)
                act.activation(acc[0:n, i, :], acc[0:n, i, :], ACT.Identity, scale=std3[0:n, i:i + 1],
                               bias=shift3[0:n, i:i + 1]).then_inc(fin_norm, 1)

        @block.tensor
        def _(pe):
            pe.wait_ge(consts_ready, N_CONSTS)
            for job, (i, half) in enumerate(IN_JOBS):
                c0 = half * 4
                dst = ps[job % 8][:, :].rearrange("p (c n) -> p c n", c=4)
                if job >= 8:
                    pe.wait_ge(evac_v, job - 7)
                if i == "pool":
                    pe.wait_ge(spool_landed, 16)
                    n = SB * PCTX
                    for c in range(4):
                        last = pe.transpose(dst[:, c, 0:n], spool[0:n, (c0 + c) * P:(c0 + c + 1) * P], ident[0:n, 0:n])
                elif i == "vec":
                    pe.wait_ge(vec_landed, 16 * 12)
                    pe.transpose(ps[0][:, 0:104], vrows[0:104, 0, :], ident[0:104, 0:104])
                    for k in range(2):
                        last = pe.transpose(ps[0][:, 104 + 124 * k:228 + 124 * k], vrows[0:124, 1 + k, :],
                                            ident[0:124, 0:124])
                else:
                    pe.wait_ge(x_landed[i], 16 if i == 1 else 32)
                    n = IN_ROWS[i]
                    for c in range(4):
                        last = pe.transpose(dst[:, c, 0:n], xin[0:n, i, (c0 + c) * P:(c0 + c + 1) * P], ident[0:n, 0:n])
                last.then_inc(turned, 1)
            pe.wait_ge(poolw_landed, 16)
            pe.wait_ge(evac_a, A_IN)
            for g in range(4):
                pe.wait_ge(d_ready, g + 1)
                for e in range(2):
                    for c in range(2):
                        last = pe.matmul(ps[2 * g + e][:, 0:NT], poolw[:, g, c, e * P:(e + 1) * P],
                                         dT[:, 2 * g + c, :], start=(c == 0), stop=(c == 1))
                    last.then_inc(pooled, 1)

            def norm(L):
                z, n, g, b = norms[L]
                if L == 1 or L == 3:
                    pe.wait_ge(z_done, KC * L + 2)
                for c in range(KC):
                    pe.wait_ge(z_done, KC * L + c + 1)
                    last = pe.matmul(ps[0][:, 0:n], mean_mat[:], z(c), start=(c == 0), stop=(c == KC - 1))
                last.then_inc(mean_done, 1)
                for c in range(KC):
                    pe.wait_ge(sq_done, KC * L + c + 1)
                    last = pe.matmul(ps[1][:, 0:n], mean_mat[:], sq[:, c, 0:n], start=(c == 0), stop=(c == KC - 1))
                last.then_inc(var_done, 1)

            def feature_block(bank, n, t, s, x_base):
                wh, wl = wide(w_hi[t % SPLIT]), wide(w_lo[t % SPLIT])
                cols = slice(s * P, (s + 1) * P)
                for c in range(KC):
                    if x_base is not None:
                        pe.wait_ge(xlo_done, x_base + c + 1)
                    for k, (w, x) in enumerate(((wh, x_hi), (wh, x_lo), (wl, x_hi))):
                        last = pe.matmul(bank[:, 0:n], w[:, c, cols], x[:, c, 0:n],
                                         start=(c == 0 and k == 0), stop=(c == KC - 1 and k == 2))
                return last

            norm(0)
            for i in range(NJ):
                for kind in range(2):
                    t = 2 * i + kind
                    pe.wait_ge(split_ready, t + 1)
                    for s in range(2):
                        q = 2 * i + s
                        if q >= 4:
                            pe.wait_ge(h_done, q - 3)
                        last = feature_block(ps[2 * (q % 4) + kind], NT, t, s, 0 if t == 0 and s == 0 else None)
                    last.then_inc(tile_used, 1)
            pe.wait_ge(h_done, FC)
            for i in range(NJ):
                t = T_DOWN + i
                pe.wait_ge(split_ready, t + 1)
                pe.wait_ge(jlo_done, i + 1)
                wh, wl = tall(w_hi[t % SPLIT]), tall(w_lo[t % SPLIT])
                for s in range(TR):
                    for c in range(KC):
                        cols = slice(c * P, (c + 1) * P)
                        for k, (w, x) in enumerate(((wh, h_hi), (wh, h_lo), (wl, h_hi))):
                            last = pe.matmul(ps[c][:, 0:NT], w[:, s, cols], x[i % 2][:, s, :],
                                             start=(i == 0 and s == 0 and k == 0),
                                             stop=(i == NJ - 1 and s == TR - 1 and k == 2))
                        if i == NJ - 1 and s == TR - 1 and c < KC - 1:
                            last.then_inc(down_done, 1)
                last.then_inc(tile_used, 1)
            norm(1)
            pe.wait_ge(sconv_landed, 32)
            pe.wait_ge(z_done, 2 * KC)
            for k, (i, half) in enumerate(CONV_JOBS):
                n = 4 * CCTX
                for c in range(4):
                    f = 4 * half + c
                    last = pe.transpose(ps[2 + k][:, c * P:c * P + n], sconv[0:n, i, f * P:(f + 1) * P], ident[0:n, 0:n])
                last.then_inc(turned, 1)
            pe.wait_ge(evac_a, A_CONV)
            for i in range(NW1 // 2):
                for kind in range(2):
                    t = T_W1 + 2 * i + kind
                    pe.wait_ge(split_ready, t + 1)
                    for s in range(2):
                        q = 2 * i + s
                        if q >= 4:
                            pe.wait_ge(u_done, q - 3)
                        last = feature_block(ps[2 * (q % 4) + kind], NT, t, s, KC if i == kind == s == 0 else None)
                    last.then_inc(tile_used, 1)
            pe.wait_ge(u_done, KC)
            for k, (part, half) in enumerate(U_JOBS):
                for c in range(4):
                    f = 4 * half + c
                    src = uext[:, f, UP - CCTX:UP] if part == 0 else uext[:, f, UP + CCTX * SB:UEXT]
                    n = (CCTX, NS)[part]
                    last = pe.transpose(ps[2 + k][0:n, c * P:(c + 1) * P], src, ident[:])
                last.then_inc(turned, 1)
            norm(2)
            pe.wait_ge(evac_a, A_U)
            for i in range(NW2):
                t = T_W2 + i
                pe.wait_ge(split_ready, t + 1)
                for s in range(2):
                    last = feature_block(ps[2 * i + s], NM, t, s, 2 * KC if i == 0 and s == 0 else None)
                last.then_inc(tile_used, 1)
            norm(3)
            pe.wait_ge(router_landed, 16)
            pe.wait_ge(y_done, 4 * KC)
            pe.wait_ge(z_done, 4 * KC)
            for i in range(3):
                n = OUT_ROWS[i]
                for c in range(KC):
                    last = pe.matmul(ps[2][0:n, i * E:(i + 1) * E], zT[:, c, META + P * i:META + P * i + n],
                                     router[:, c, :], start=(c == 0), stop=(c == KC - 1))
            last.then_inc(routed, 1)
            for k, (i, half) in enumerate(X_JOBS):
                n = OUT_ROWS[i]
                for c in range(4):
                    f = 4 * half + c
                    last = pe.transpose(ps[(3 + k) % 8][0:n, c * P:(c + 1) * P],
                                        zT[:, f, META + P * i:META + P * i + n], ident[:])
                last.then_inc(turned, 1)
            pe.wait_ge(mask_ready, 1)
            for i in range(3):
                for k in range(i + 1):
                    n = OUT_ROWS[k]
                    pe.matmul(ps[1][:, i * E:(i + 1) * E], (before if k == i else ones)[0:n, :], taken[0:n, k, :],
                              start=(k == 0), stop=(k == i))
            for k in range(3):
                n = OUT_ROWS[k]
                last = pe.matmul(ps[1][:, 3 * E:4 * E], ones[0:n, :], taken[0:n, k, :], start=(k == 0), stop=(k == 2))
            last.then_inc(placed, 1)

            def gather(g):
                pe.wait_ge(sel_ready, g + 1)
                for k in range(2):
                    for c in range(4):
                        f = (4 * k + c) * P
                        for m in range(6):
                            x, i = (xn_hi, xn_lo)[m % 2], m // 2
                            last = pe.matmul(ps[1 + 2 * k][:, c * P:(c + 1) * P], x[:, i, f:f + P], sel[:, i, :],
                                             start=(m == 0), stop=(m == 5))
                    last.then_inc(gathered, 1)

            SCATTER_BANKS = (4, 5, 1, 3, 4, 5)

            def scatter(done, y_count):
                pe.wait_ge(yy_lo_done, y_count)
                for k in range(6):
                    i, half = k // 2, k % 2
                    n = OUT_ROWS[i]
                    if k >= 4:
                        pe.wait_ge(summed, done + (k - 3))
                    for m, y in enumerate((yy_hi, yy_lo)):
                        last = pe.matmul(ps[SCATTER_BANKS[k]][0:n, :], sel_t[:, P * i:P * i + n],
                                         y[:, half * HALF:(half + 1) * HALF], start=(m == 0), stop=(m == 1))
                    last.then_inc(spread, 1)

            def one_pass(r):
                gather(r * RTOT)
                with pe.Fori(0, E) as e:
                    n = r * E + e
                    scattered = r * SCAT + e * 6

                    def rows_block(bank, j, t):
                        pe.wait_ge(split_ready, n * TE + (t + 1))
                        wh, wl = wide(w_hi[t % SPLIT]), wide(w_lo[t % SPLIT])
                        for c in range(KC):
                            for k, (x, w) in enumerate(((xg_hi, wh), (xg_hi, wl), (xg_lo, wh))):
                                last = pe.matmul(bank[:, 0:TW], x[:, c, :], w[:, c, :],
                                                 start=(c == 0 and k == 0), stop=(c == KC - 1 and k == 2))
                        last.then_inc(tile_used, 1)

                    def turn_h(j):
                        pe.wait_ge(h_done, n * NJ + (FC + j + 1))
                        if j >= 2:
                            pe.wait_ge(ht_lo_done, n * NJ + (j - 1))
                        for s in range(TR):
                            last = pe.transpose(ps[4 + j % 2][:, s * P:(s + 1) * P], hn[:, s * P:(s + 1) * P], ident[:])
                        last.then_inc(h_turned, 1)

                    def down(j, t):
                        pe.wait_ge(split_ready, n * TE + (t + 1))
                        pe.wait_ge(ht_lo_done, n * NJ + (j + 1))
                        wh, wl = tall(w_hi[t % SPLIT]), tall(w_lo[t % SPLIT])
                        for s in range(TR):
                            for half in range(2):
                                cols = slice(half * HALF, (half + 1) * HALF)
                                for k, (x, w) in enumerate(((ht_hi, wh), (ht_hi, wl), (ht_lo, wh))):
                                    last = pe.matmul(ps[6 + half][:, :], x[:, s, :], w[:, s, cols],
                                                     start=(j == 0 and s == 0 and k == 0),
                                                     stop=(j == NJ - 1 and s == TR - 1 and k == 2))
                        last.then_inc(tile_used, 1)

                    for j in range(NJ):
                        g = T_MOE + (3 * j - 1 if j else 0)
                        if j == 0:
                            pe.wait_ge(xg_lo_done, (r * RTOT + e) * 2 + 2)
                        if j == 1:
                            pe.wait_ge(summed, scattered + 6)
                        pe.wait_ge(silu_done, n * NJ + (FC + max(0, j - 1)))
                        rows_block(ps[j % 2], j, g)
                        if j >= 1:
                            turn_h(j - 1)
                        if j == 1:
                            for i in range(3):
                                m = OUT_ROWS[i]
                                last = pe.transpose(ps[5][:, P * i:P * i + m], sel[0:m, i, :].bitcast(F32),
                                                    ident[0:m, 0:m])
                            last.then_inc(sel_turned, 1)
                        if j == 2:
                            pe.wait_ge(sel_t_done, n + 1)
                        pe.wait_ge(h_done, n * NJ + (FC + max(0, j - 1)))
                        rows_block(ps[2 + j % 2], j, g + 1)
                        if j == 0:
                            scatter(scattered, n * 2 + 2)
                        else:
                            down(j - 1, g + 2)
                    turn_h(NJ - 1)
                    gather(r * RTOT + e + 1)
                    down(NJ - 1, T_MOE + TE - 1)
                scatter(r * SCAT + 6 * E, (r * E + E) * 2 + 2)

            pe.wait_ge(acc_ready, 6)
            pe.wait_ge(xlo_done, 3 * KC + 6)
            one_pass(0)
            pe.wait_ge(flag_ready, 1)
            largest = pe.value_load(most_i[0:1, 0:1], min_val=0, max_val=NM)
            with pe.If(largest > P):
                with pe.Fori(1, 3) as r:
                    one_pass(r)

        @block.vector
        def _(dve):
            steps = [0]

            def link(ins):
                steps[0] += 1
                ins.then_inc(dve_step, 1)
                dve.wait_ge(dve_step, steps[0])

            def lo(t, n=None):
                dve.wait_ge(hi_ready, t + 1 if n is None else n * TE + (t + 1))
                dve.tensor_tensor(w_lo[t % SPLIT][:], raw[t % RAW][:], w_hi[t % SPLIT][:],
                                  ALU.subtract).then_inc(split_ready, 1)

            for job, (i, half) in enumerate(IN_JOBS):
                src = ps[job % 8][:, :].rearrange("p (c n) -> p c n", c=4)
                if half == 0 and i in (0, 1):
                    dve.wait_ge(turned, job + 1)
                    dve.tensor_copy(pext[:, 0:4, PCTX + P * i:PCTX + P * (i + 1)], src).then_inc(evac_v, 1)
                elif half == 0 and i == 2:
                    dve.wait_ge(turned, job + 1)
                    dve.tensor_copy(pext[:, 0:4, PCTX + 2 * P:PCTX + NPR], src[:, :, 0:META])
                    for c in range(4):
                        last = dve.tensor_copy(pext_s[:, c, :, PCTX:PCTX + ST_],
                                               src[:, c, META:META + NS].rearrange("p (b j) -> p b j", b=SB))
                    last.then_inc(evac_v, 1)
            dve.wait_ge(consts_ready, N_CONSTS)
            link(dve.tensor_scalar(recip[:], slot_no[:, 0:16], 1.0, None, ALU.add))
            link(dve.reciprocal(recip[:], recip[:]))
            dve.wait_ge(turned, VEC_JOB + 1)
            dve.tensor_copy(vec[:], ps[0][:, 0:104 + KC * TAPS]).then_inc(evac_v, 1)
            dve.wait_ge(evac_v, 4)
            dve.wait_ge(evac_a, A_IN)
            dve.wait_ge(ctx_zeroed, 1)
            for g, w in enumerate(WINDOWS):
                x = pext[:, 2 * g:2 * g + 2, :]
                if g:
                    dve.wait_ge(d_ready, g)
                cur, other, have = win_a, win_b, 2
                link(dve.tensor_tensor(cur[:, :, 1:PEXT], x[:, :, 1:PEXT], x[:, :, 0:PEXT - 1], ALU.add))
                while have < w:
                    lo_col = 2 * have - 1
                    link(dve.tensor_tensor(other[:, :, lo_col:PEXT], cur[:, :, lo_col:PEXT],
                                           cur[:, :, lo_col - have:PEXT - have], ALU.add))
                    cur, other, have = other, cur, 2 * have
                out = dT[:, 2 * g:2 * g + 2, :]
                link(dve.scalar_tensor_tensor(out=out[:, :, 0:NPR], in0=cur[:, :, PCTX:PCTX + NPR], scalar=1.0 / w,
                                              in1=x[:, :, PCTX:PCTX + NPR], op0=ALU.mult, op1=ALU.subtract))
                for c in range(2):
                    link(dve.tensor_tensor(out[:, c, 0:w], cur[:, c, PCTX:PCTX + w], recip[:, 0:w], ALU.mult))
                    link(dve.tensor_tensor(out[:, c, 0:w], out[:, c, 0:w], x[:, c, PCTX:PCTX + w], ALU.subtract))
                    cur_s = cur[:, c, PCTX + NPR:PEXT].rearrange("p (b j) -> p b j", b=SB)[:, :, PCTX:PCTX + ST_]
                    last = dve.scalar_tensor_tensor(
                        out=out[:, c, NPR:NT].rearrange("p (b j) -> p b j", b=SB), in0=cur_s, scalar=1.0 / w,
                        in1=pext_s[:, 2 * g + c, :, PCTX:PCTX + ST_], op0=ALU.mult, op1=ALU.subtract)
                last.then_inc(d_ready, 1)
            dve.wait_ge(resid_ready, 1)
            for c in range(KC):
                dve.wait_ge(pooled, c + 1)
                dve.scalar_tensor_tensor(out=zT[:, c, :], in0=ps[c][:, 0:NT], scalar=v(V_SCALE + c), in1=zT[:, c, :],
                                         op0=ALU.mult, op1=ALU.add).then_inc(z_done, 1)
            lo(0)
            lo(1)

            def norm(L):
                z, n, g, b = norms[L]
                dve.wait_ge(mean_done, L + 1)
                dve.wait_ge(z_done, KC * (L + 1))
                for c in range(KC):
                    dve.tensor_tensor(z(c), z(c), ps[0][:, 0:n], ALU.subtract).then_inc(xc_done, 1)
                dve.wait_ge(std_done, L + 1)
                dve.wait_ge(xc_done, KC * (L + 1))
                link(dve.reciprocal(rs[:, 0:n], rs[:, 0:n]))
                for c in range(KC):
                    dve.scalar_tensor_tensor(out=z(c), in0=z(c), scalar=v(g + c), in1=rs[:, 0:n],
                                             op0=ALU.mult, op1=ALU.mult).then_inc(yg_done, 1)

                def low(c):
                    dve.wait_ge(xhi_done, KC * L + c + 1)
                    dve.tensor_tensor(x_lo[:, c, 0:n], z(c), x_hi[:, c, 0:n], ALU.subtract).then_inc(xlo_done, 1)

                for c in range(KC):
                    dve.wait_ge(yg_done, KC * L + c + 1)
                    dve.tensor_scalar(z(c), z(c), v(b + c), None, ALU.add).then_inc(y_done, 1)
                    if L < 3 and c >= 1:
                        low(c - 1)
                if L < 3:
                    low(KC - 1)

            norm(0)
            for i in range(NJ):
                lo(2 * i + 2)
                lo(2 * i + 3)
                dve.wait_ge(tile_used, 2 * i + 2)
                for s in range(2):
                    q = 2 * i + s
                    dve.wait_ge(silu_done, q + 1)
                    dve.tensor_tensor(h[:, q, :], sg[s][:], ps[2 * (q % 4) + 1][:, 0:NT], ALU.mult).then_inc(h_done, 1)
            for i in range(-1, NJ):
                if i >= 0:
                    lo(T_DOWN + i + 2)
                if i + 1 < NJ:
                    k = (i + 1) % 2
                    dve.wait_ge(jhi_done, i + 2)
                    if i < 0:
                        dve.wait_ge(h_done, FC)
                    dve.tensor_tensor(h_lo[k][:], h[:, 2 * i + 2:2 * i + 4, :], h_hi[k][:],
                                      ALU.subtract).then_inc(jlo_done, 1)
            for c in range(KC):
                if c < KC - 1:
                    dve.wait_ge(down_done, c + 1)
                else:
                    dve.wait_ge(tile_used, T_W1)
                dve.wait_ge(scaled, c + 1)
                dve.tensor_tensor(zT[:, c, :], zT[:, c, :], ps[c][:, 0:NT], ALU.add).then_inc(z_done, 1)
            norm(1)
            dve.wait_ge(ctx_zeroed, 2)
            dve.wait_ge(evac_a, A_CONV)
            taps_done = 0
            for i in range(NW1 // 2):
                lo(T_W1 + 2 * i + 2)
                lo(T_W1 + 2 * i + 3)
                for s in range(2):
                    q = 2 * i + s
                    dve.wait_ge(sig_done, q + 1)
                    src = ps[2 * (q % 4)]
                    dve.scalar_tensor_tensor(out=uext[:, q, CCTX:UP], in0=src[:, 0:NPR], scalar=v(V_B1 + q),
                                             in1=sg[s][:, 0:NPR], op0=ALU.add, op1=ALU.mult)
                    dve.scalar_tensor_tensor(out=uext_s[:, q, :, CCTX:CCTX + ST_],
                                             in0=src[:, NPR:NT].rearrange("p (b j) -> p b j", b=SB), scalar=v(V_B1 + q),
                                             in1=sg[s][:, NPR:NT].rearrange("p (b j) -> p b j", b=SB),
                                             op0=ALU.add, op1=ALU.mult).then_inc(u_done, 1)
                dve.wait_ge(u_done, 2 * i + 2)
                last_of = {}
                for k in range(TAPS):
                    for s in range(2):
                        q = 2 * i + s
                        w = v(V_DW + KC * k + q)
                        for part in range(2):
                            if part == 0:
                                out, src = cacc[:, q, 0:SEQ], uext[:, q, META + k:META + k + SEQ]
                            else:
                                out = cacc[:, q, SEQ:NM].rearrange("p (b j) -> p b j", b=SB)
                                src = uext_s[:, q, :, k:k + ST_]
                            if k == 0:
                                ins = dve.tensor_scalar(out, src, w, v(V_DWB + q), ALU.mult, ALU.add)
                            else:
                                dve.wait_ge(conv_step, last_of[s, part])
                                ins = dve.scalar_tensor_tensor(out=out, in0=src, scalar=w, in1=out,
                                                               op0=ALU.mult, op1=ALU.add)
                            if k == TAPS - 1 and part == 1:
                                ins.then_inc(z_done, 1)
                            else:
                                taps_done += 1
                                last_of[s, part] = taps_done
                                ins.then_inc(conv_step, 1)
            norm(2)
            for i in range(NW2):
                lo(T_W2 + 2 + i)
                dve.wait_ge(tile_used, T_W2 + i + 1)
                for s in range(2):
                    q = 2 * i + s
                    dve.wait_ge(scaled, KC + q + 1)
                    dve.tensor_tensor(zT[:, q, META:NT], zT[:, q, META:NT], ps[q][:, 0:NM], ALU.add).then_inc(z_done, 1)
            norm(3)
            dve.wait_ge(routed, 1)
            for i in range(3):
                n = OUT_ROWS[i]
                last = dve.tensor_copy(logits[0:n, i, :], ps[2][0:n, i * E:(i + 1) * E])
            link(last)
            for i in range(3):
                last = dve.max(top_v[:, i, :], logits[:, i, :])
            link(last)
            for i in range(3):
                last = dve.max_index(top_i[:, i, :], top_v[:, i, :], logits[:, i, :])
            link(last)
            dve.tensor_tensor(prob[:, :, 0:1], top_v[:, :, 1:2], top_v[:, :, 0:1], ALU.subtract).then_inc(gap_ready, 1)
            link(dve.tensor_copy(top_f[:], top_i[:, :, 0:2]))
            for i in range(3):
                for k, pick in enumerate((pick1, pick2)):
                    last = dve.tensor_scalar(pick[:, i, :], slot_no[:, 0:E], top_f[:, i, k:k + 1], None, ALU.is_equal)
            link(last)
            for i in range(3):
                n = OUT_ROWS[i]
                last = dve.tensor_tensor(taken[0:n, i, :], pick1[0:n, i, :], pick2[0:n, i, :], ALU.add)
            last.then_inc(mask_ready, 1)
            dve.wait_ge(exp_done, 1)
            link(dve.tensor_scalar(prob[:, :, 2:3], prob[:, :, 1:2], 1.0, None, ALU.add))
            link(dve.reciprocal(prob[:, :, 2:3], prob[:, :, 2:3]))
            link(dve.tensor_tensor(prob[:, :, 3:4], prob[:, :, 1:2], prob[:, :, 2:3], ALU.mult))
            for i in range(3):
                last = dve.tensor_scalar(pick1[:, i, :], pick1[:, i, :], prob[:, i, 2:3], None, ALU.mult)
            link(last)
            for i in range(3):
                n = OUT_ROWS[i]
                last = dve.scalar_tensor_tensor(out=gate[0:n, i, 1:1 + E], in0=pick2[0:n, i, :],
                                                scalar=prob[0:n, i, 3:4], in1=pick1[0:n, i, :],
                                                op0=ALU.mult, op1=ALU.add)
            link(last)
            dve.wait_ge(placed, 1)
            dve.wait_ge(mask_ready, 1)
            for i in range(3):
                last = dve.scalar_tensor_tensor(out=slot_of[:, i, 0:E], in0=ps[1][:, i * E:(i + 1) * E], scalar=1.0,
                                                in1=taken[:, i, :], op0=ALU.add, op1=ALU.mult)
            link(last)
            link(dve.tensor_scalar(slot_of[:, :, 0:E], slot_of[:, :, 0:E], 1.0, None, ALU.subtract))
            link(dve.tensor_reduce(most[:], ps[1][:, 3 * E:4 * E], AX.X, ALU.max))
            dve.tensor_copy(most_i[:], most[:]).then_inc(flag_ready, 1)

            def select(e, count):
                for i in range(3):
                    last = dve.tensor_scalar(sel[:, i, :], slot_no[:], slot_of[:, i, bass.ds(e, 1)], None, ALU.is_equal)
                last.then_inc(sel_ready, 1)

            dve.wait_ge(turned, T_XJ + len(X_JOBS))
            select(0, 0)
            dve.memset(sel_t[:].bitcast(F32), 0.0)
            dve.memset(yy_hi[:].bitcast(F32), 0.0).then_inc(yy_lo_done, 1)
            dve.memset(yy_lo[:].bitcast(F32), 0.0).then_inc(yy_lo_done, 1)
            for k, (i, half) in enumerate(X_JOBS):
                n = OUT_ROWS[i]
                dve.wait_ge(xhi_done, 3 * KC + k + 1)
                if i == 2:
                    dve.wait_ge(ctx_zeroed, 4)
                cols = slice(half * HALF, (half + 1) * HALF)
                dve.tensor_tensor(xn_lo[0:n, i, cols], ps[(3 + k) % 8][0:n, :], xn_hi[0:n, i, cols],
                                  ALU.subtract).then_inc(xlo_done, 1)

            SCATTER_BANKS = (4, 5, 1, 3, 4, 5)

            def add_scattered(col, done):
                for k in range(6):
                    i, half = k // 2, k % 2
                    n = OUT_ROWS[i]
                    cols = slice(half * HALF, (half + 1) * HALF)
                    dve.wait_ge(spread, done + (k + 1))
                    dve.scalar_tensor_tensor(out=acc[0:n, i, cols], in0=ps[SCATTER_BANKS[k]][0:n, :],
                                             scalar=gate[0:n, i, bass.ds(col, 1)], in1=acc[0:n, i, cols],
                                             op0=ALU.mult, op1=ALU.add).then_inc(summed, 1)

            def xg_low(g):
                for k in range(2):
                    dve.wait_ge(xg_hi_done, 2 * g + (k + 1))
                    dve.tensor_tensor(xg_lo[:, 4 * k:4 * k + 4, :],
                                      ps[1 + 2 * k][:, :].rearrange("p (c n) -> p c n", c=4),
                                      xg_hi[:, 4 * k:4 * k + 4, :], ALU.subtract).then_inc(xg_lo_done, 1)

            def one_pass(r):
                xg_low(r * RTOT)
                with dve.Fori(0, E) as e:
                    n = r * E + e

                    def mult(j, up_tile):
                        dve.wait_ge(silu_done, n * NJ + (FC + j + 1))
                        dve.wait_ge(tile_used, n * TE + (T_MOE + up_tile + 1))
                        dve.tensor_tensor(hn[:], sgn[:], ps[2 + j % 2][:, 0:TW], ALU.mult).then_inc(h_done, 1)

                    def turn_low(j):
                        dve.wait_ge(ht_hi_done, n * NJ + (j + 1))
                        dve.tensor_tensor(ht_lo[:], ps[4 + j % 2][:, 0:TR * P].rearrange("p (c n) -> p c n", c=TR),
                                          ht_hi[:], ALU.subtract).then_inc(ht_lo_done, 1)

                    lo(T_MOE + 2, n)
                    lo(T_MOE + 3, n)
                    mult(0, 1)
                    dve.wait_ge(h_done, n * NJ + (FC + 1))
                    add_scattered(e, r * SCAT + e * 6)
                    for j in range(1, NJ):
                        g = 3 * j - 1
                        lo(T_MOE + g + 2, n)
                        turn_low(j - 1)
                        lo(T_MOE + g + 3, n)
                        mult(j, g + 1)
                        lo(T_MOE + g + 4, n)
                        if j == 2:
                            dve.wait_ge(sel_turned, n + 1)
                            select(e + 1, 0)
                    turn_low(NJ - 1)
                    xg_low(r * RTOT + e + 1)
                    lo(T_MOE + TE + 1, n)
                    for k in range(2):
                        dve.wait_ge(yy_hi_done, n * 2 + (k + 1))
                        cols = slice(k * HALF, (k + 1) * HALF)
                        dve.tensor_tensor(yy_lo[:, cols], ps[6 + k][:, :], yy_hi[:, cols],
                                          ALU.subtract).then_inc(yy_lo_done, 1)
                dve.wait_ge(yy_lo_done, (r * E + E) * 2 + 2)
                add_scattered(E, r * SCAT + 6 * E)
                dve.wait_ge(summed, r * SCAT + SCAT)

            dve.wait_ge(acc_ready, 6)
            one_pass(0)
            dve.wait_ge(flag_ready, 1)
            largest = dve.value_load(most_i[0:1, 0:1], min_val=0, max_val=NM)
            with dve.If(largest > P):
                with dve.Fori(1, 3) as r:
                    dve.wait_ge(gathered, r * (2 * RTOT))
                    dve.tensor_scalar(slot_of[:, :, 0:E], slot_of[:, :, 0:E], float(P), None,
                                      ALU.subtract).then_inc(slots_moved, 1)
                    dve.wait_ge(slots_moved, r)
                    select(0, 0)
                    one_pass(r)
            for i in range(3):
                n = OUT_ROWS[i]
                for k in range(2):
                    last = dve.bn_stats(stats[0:n, i, k, :], acc[0:n, i, k * HALF:(k + 1) * HALF])
                link(last)
                dve.bn_aggr(mv[0:n, i, :], stats[0:n, i, :, :].rearrange("p a b -> p (a b)")).then_inc(fin_stats, 1)
            for i in range(3):
                n = OUT_ROWS[i]
                dve.wait_ge(fin_std, i + 1)
                link(dve.reciprocal(std3[0:n, i:i + 1], std3[0:n, i:i + 1]))
                dve.scalar_tensor_tensor(out=shift3[0:n, i:i + 1], in0=mv[0:n, i, 0:1], scalar=-1.0,
                                         in1=std3[0:n, i:i + 1], op0=ALU.mult, op1=ALU.mult).then_inc(fin_recip, 1)
            dve.wait_ge(rows_landed, 32)
            for i in range(3):
                n = OUT_ROWS[i]
                dve.wait_ge(fin_norm, i + 1)
                dve.tensor_tensor(acc[0:n, i, :], acc[0:n, i, :], g_row[0:n, :], ALU.mult).then_inc(fin_g, 1)
                dve.wait_ge(fin_g, i + 1)
                dve.tensor_tensor(acc[0:n, i, :], acc[0:n, i, :], b_row[0:n, :], ALU.add).then_inc(fin_out, 1)



_INS = ['x_prompt', 'x_sample', 'state_pool', 'state_conv', 'meta', 'pool_w', 'pool_scale', 'conv_w1', 'conv_b1',
        'conv_dw', 'conv_dw_b', 'conv_ln_g', 'conv_ln_b', 'conv_w2', 'conv_b2', 'ln_mix_g', 'ln_mix_b', 'ln_ffn_g',
        'ln_ffn_b', 'ffn_w_gate', 'ffn_w_up', 'ffn_w_down', 'moe_router', 'moe_w_gate', 'moe_w_up', 'moe_w_down']
_OUTS = [((1, 256, 1024), 'float32'), ((8, 4, 1024), 'float32'), ((1, 1, 15, 1024), 'float32'),
         ((1, 1, 30, 1024), 'float32'), ((1, 8, 15, 1024), 'float32'), ((1, 8, 30, 1024), 'float32')]


def kernel(**inputs):
    import numpy as _np
    import concourse.bacc as _bacc
    from concourse import mybir as _mybir
    from concourse.bass_utils import run_bass_kernel_spmd as _run

    nc = _bacc.Bacc("TRN2", target_bir_lowering=False, num_devices=1)
    arrays, args = {}, []
    for name in _INS:
        a = _np.ascontiguousarray(inputs[name])
        arrays[f"in_{name}_dram"] = a
        args.append(nc.dram_tensor(f"in_{name}_dram", a.shape, _mybir.dt.from_np(a.dtype), kind="ExternalInput").ap())
    for i, (shape, dtype) in enumerate(_OUTS):
        dt = _mybir.dt.from_np(_np.dtype(dtype))
        args.append(nc.dram_tensor(f"out_{i}_dram", shape, dt, kind="ExternalOutput").ap())
    build_trunk(nc, *args)
    r = _run(nc, [arrays], core_ids=[0])
    return tuple(r.results[0][f"out_{i}_dram"] for i in range(len(_OUTS)))
```

```python
from contextlib import ExitStack

import concourse.bass as bass
from concourse import mybir

F32 = mybir.dt.float32
F32R = mybir.dt.float32r
I32 = mybir.dt.int32
U32 = mybir.dt.uint32
ALU = mybir.AluOpType
ACT = mybir.ActivationFunctionType
AX = mybir.AxisListType

P = 128
RAW = 11
SPLIT = 3
LN_EPS = 1e-5
WINDOWS = (2, 4, 8, 16)
NEG = -1.0


def build_trunk(nc, x_prompt, x_sample, state_pool, state_conv, meta, pool_w, pool_scale, conv_w1,
                conv_b1, conv_dw, conv_dw_b, conv_ln_g, conv_ln_b, conv_w2, conv_b2, ln_mix_g,
                ln_mix_b, ln_ffn_g, ln_ffn_b, ffn_w_gate, ffn_w_up, ffn_w_down, moe_router,
                moe_w_gate, moe_w_up, moe_w_down, y_prompt, y_sample, new_pool_prompt,
                new_conv_prompt, new_pool_sample, new_conv_sample):
    D = x_prompt.shape[2]
    KC = D // P
    SEQ = x_prompt.shape[1]
    SB, ST_ = x_sample.shape[:2]
    META = meta.shape[0]
    PCTX = state_pool.shape[2]
    CCTX = state_conv.shape[2]
    TAPS = conv_dw.shape[1]
    F = ffn_w_gate.shape[2]
    E = moe_router.shape[2]
    NPR = META + SEQ
    NS = SB * ST_
    NT = NPR + NS
    NM = SEQ + NS
    ALPHA = float(4) ** 0.25
    HALF = D // 2
    TW = 256
    TR = 2
    NJ = F // TW
    FC = F // P
    IN_ROWS = (P, P, NT - 2 * P)
    OUT_ROWS = (P, P, NM - 2 * P)
    T_DOWN = 2 * NJ
    T_W1 = 3 * NJ
    NW1 = 2 * D // TW
    T_W2 = T_W1 + NW1
    NW2 = D // TW
    T_MOE = T_W2 + NW2
    TE = 3 * NJ
    assert TE % RAW == 0 and TE % SPLIT == 0

    with ExitStack() as ctx:
        ring_at = 16512
        split_at = ring_at + RAW * 8192
        const_at = split_at + 2 * SPLIT * 8192
        place = [const_at]

        def at(name, shape, dt, offset):
            assert offset % 32 == 0, (name, offset)
            return nc.alloc_sbuf_tensor_at(name, shape, dt, offset=offset)

        def const(name, shape, dt=F32):
            n = 4
            for s in shape[1:]:
                n *= s
            t = at(name, shape, dt, place[0])
            place[0] += (n + 31) // 32 * 32
            return t

        raw = [at(f"raw{i}", [P, 2048], F32, ring_at + 8192 * i) for i in range(RAW)]
        w_hi = [at(f"w_hi{i}", [P, 2048], F32R, split_at + 16384 * i) for i in range(SPLIT)]
        w_lo = [at(f"w_lo{i}", [P, 2048], F32R, split_at + 16384 * i + 8192) for i in range(SPLIT)]

        ident = const("ident", [P, P])
        mean_mat = const("mean_mat", [P, P])
        ones = const("ones", [P, P])
        before = const("before", [P, P])
        slot_no = const("slot_no", [P, P])
        vec = const("vec", [P, 104 + KC * TAPS])
        eps = const("eps", [P, 1])
        router = const("router", [P, KC, E])
        logits = const("logits", [P, 3, E])
        top_v = const("top_v", [P, 3, 8])
        top_i = const("top_i", [P, 3, 8], U32)
        top_f = const("top_f", [P, 3, 2])
        prob = const("prob", [P, 3, 4])
        pick1 = const("pick1", [P, 3, E])
        pick2 = const("pick2", [P, 3, E])
        taken = const("taken", [P, 3, E])
        gate = const("gate", [P, 3, 1 + E])
        slot_of = const("slot_of", [P, 3, E + 1])
        most = const("most", [P, 1])
        most_i = const("most_i", [P, 1], I32)
        mv = const("mv", [P, 3, 2])
        std3 = const("std3", [P, 3])
        work = place[0]
        end = 229368

        def area(name, shape, dt, offset):
            n = 4
            for s in shape[1:]:
                n *= s
            assert work + offset + n <= end, (name, work + offset + n - end)
            return at(name, shape, dt, work + offset)

        XB = KC * NT * 4
        zT = area("zT", [P, KC, NT], F32, 0)
        x_hi = area("x_hi", [P, KC, NT], F32R, XB)
        x_lo = area("x_lo", [P, KC, NT], F32R, 2 * XB)
        A3 = 3 * XB
        PEXT = PCTX + NPR + SB * (PCTX + ST_)
        pext = area("pext", [P, KC, PEXT], F32, A3)
        dT = area("dT", [P, KC, NT], F32, A3 + KC * PEXT * 4)
        sq = area("sq", [P, KC, NT], F32, A3)
        FIRST_BORROWED = 6
        slot = lambda i: ring_at + 8192 * i
        win_a = at("win_a", [P, 2, PEXT], F32, slot(6))
        win_b = at("win_b", [P, 2, PEXT], F32, slot(6) + 3520)
        recip = at("recip", [P, 16], F32, slot(6) + 7168)
        xin = at("xin", [P, 3, D], F32, slot(7))
        spool = at("spool", [P, D], F32, slot(8) + 4096)
        poolw = at("poolw", [P, 4, 2, 256], F32, slot(9))
        vrows = at("vrows", [P, 3, P], F32, slot(10))
        h = area("h", [P, FC, NT], F32, A3)
        JB = A3 + FC * NT * 4
        h_hi = [area(f"h_hi{i}", [P, 2, NT], F32R, JB + 4864 * i) for i in range(2)]
        h_lo = [area(f"h_lo{i}", [P, 2, NT], F32R, JB + 4864 * i + 2432) for i in range(2)]
        sg = [area(f"sg{i}", [P, NT], F32, JB + 9728 + 1216 * i) for i in range(2)]
        rs = sg[0]
        UP = CCTX + NPR
        UEXT = UP + SB * (CCTX + ST_)
        uext = area("uext", [P, KC, UEXT], F32, A3)
        A4 = A3 + KC * UEXT * 4
        sconv = area("sconv", [P, 2, D], F32, A4)
        unat = area("unat", [32, 2, D], F32, A4)
        cacc = area("cacc", [P, KC, NM], F32, A4 + 8192)
        NPE = KC // 2
        Q0 = KC - NPE
        UW = SEQ + CCTX
        uc_hi = area("uc_hi", [P, NPE, UW], F32R, XB)
        uc_lo = area("uc_lo", [P, NPE, UW], F32R, XB + NPE * UW * 4)
        prod = area("prod", [P, 2, NS, TAPS], F32, 2 * XB)
        dw_lo = area("dw_lo", [P, TAPS, NPE], F32, A4 + 8192 + KC * NM * 4)
        dw_hi = area("dw_hi", [P, TAPS, NPE], F32R, A4 + 8192 + (KC - 1) * NM * 4)
        M0 = XB
        xn_hi = area("xn_hi", [P, 3, D], F32R, M0)
        xn_lo = area("xn_lo", [P, 3, D], F32R, M0 + 12288)
        acc = area("acc", [P, 3, D], F32, M0 + 24576)
        M1 = M0 + 36864
        xg_hi = area("xg_hi", [P, KC, P], F32R, M1)
        xg_lo = area("xg_lo", [P, KC, P], F32R, M1 + 4096)
        hn = area("hn", [P, TW], F32, M1 + 8192)
        stats = area("stats", [P, 3, 2, 6], F32, M1 + 8192)
        sgn = area("sgn", [P, TW], F32, M1 + 9216)
        ht_hi = area("ht_hi", [P, TR, P], F32R, M1 + 10240)
        ht_lo = area("ht_lo", [P, TR, P], F32R, M1 + 11264)
        sel_t = area("sel_t", [P, NM], F32R, M1 + 12288)
        g_row = area("g_row", [P, D], F32, M1 + 13440)
        b_row = area("b_row", [P, D], F32, M1 + 17536)
        yy_hi = area("yy_hi", [P, D], F32R, 0)
        yy_lo = area("yy_lo", [P, D], F32R, 4096)
        xg_rows = area("xg_rows", [P, D], F32, 0)
        sel = area("sel", [P, 3, P], F32R, 8192)

        ps = [ctx.enter_context(nc.psum_tensor(f"bank{i}", [P, 512], F32)) for i in range(8)]

        def sem(name):
            return ctx.enter_context(nc.semaphore(name))

        raw_landed = [sem(f"raw_landed{i}") for i in range(RAW)]
        x_landed = [sem(f"x_landed{i}") for i in range(3)]
        spool_landed = sem("spool_landed")
        poolw_landed = sem("poolw_landed")
        vec_landed = sem("vec_landed")
        router_landed = sem("router_landed")
        sconv_landed = sem("sconv_landed")
        rows_landed = sem("rows_landed")
        stored = sem("stored")
        u_stored = sem("u_stored")
        hi_ready = sem("hi_ready")
        split_ready = sem("split_ready")
        tile_used = sem("tile_used")
        consts_ready = sem("consts_ready")
        ctx_zeroed = sem("ctx_zeroed")
        turned = sem("turned")
        evac_v = sem("evac_v")
        evac_a = sem("evac_a")
        dve_step = sem("dve_step")
        act_step = sem("act_step")
        pool_step = sem("pool_step")
        d_ready = sem("d_ready")
        resid_ready = sem("resid_ready")
        scaled = sem("scaled")
        pooled = sem("pooled")
        z_done = sem("z_done")
        mean_done = sem("mean_done")
        xc_done = sem("xc_done")
        sq_done = sem("sq_done")
        var_done = sem("var_done")
        std_done = sem("std_done")
        yg_done = sem("yg_done")
        y_done = sem("y_done")
        gains_ready = sem("gains_ready")
        xhi_done = sem("xhi_done")
        xlo_done = sem("xlo_done")
        silu_done = sem("silu_done")
        h_done = sem("h_done")
        jhi_done = sem("jhi_done")
        jlo_done = sem("jlo_done")
        down_done = sem("down_done")
        sig_done = sem("sig_done")
        u_done = sem("u_done")
        conv_step = sem("conv_step")
        dw_lo_ready = sem("dw_lo_ready")
        uc_hi_done = sem("uc_hi_done")
        uc_lo_done = sem("uc_lo_done")
        diag_hi_done = sem("diag_hi_done")
        diag_lo_done = sem("diag_lo_done")
        diag_used = sem("diag_used")
        conv_out = sem("conv_out")
        prod_done = sem("prod_done")
        prod_used = sem("prod_used")
        routed = sem("routed")
        gap_ready = sem("gap_ready")
        exp_done = sem("exp_done")
        slots_moved = sem("slots_moved")
        mask_ready = sem("mask_ready")
        placed = sem("placed")
        counted = sem("counted")
        flag_ready = sem("flag_ready")
        acc_ready = sem("acc_ready")
        sel_ready = sem("sel_ready")
        rows_gathered = sem("rows_gathered")
        rows_out = sem("rows_out")
        gathered = sem("gathered")
        xg_hi_done = sem("xg_hi_done")
        xg_lo_done = sem("xg_lo_done")
        h_turned = sem("h_turned")
        ht_hi_done = sem("ht_hi_done")
        ht_lo_done = sem("ht_lo_done")
        sel_turned = sem("sel_turned")
        sel_t_done = sem("sel_t_done")
        yy_hi_done = sem("yy_hi_done")
        yy_lo_done = sem("yy_lo_done")
        yy_cleared = sem("yy_cleared")
        spread = sem("spread")
        summed = sem("summed")
        fin_half = sem("fin_half")
        fin_stats = sem("fin_stats")
        fin_std = sem("fin_std")
        fin_recip = sem("fin_recip")
        fin_g = sem("fin_g")
        fin_out = sem("fin_out")

        V_SCALE, V_B1, V_DWB, V_CG, V_CB, V_B2, V_MG, V_MB, V_FG, V_FB, V_DW = (
            0, 8, 24, 32, 40, 48, 56, 72, 88, 96, 104)

        def v(col):
            return vec[:, col:col + 1]

        def wide(t):
            return t[:, :].rearrange("p (k f) -> p k f", k=KC)

        def tall(t):
            return t[:, :].rearrange("p (k f) -> p k f", k=TR)

        pext_s = pext[:, :, PCTX + NPR:PEXT].rearrange("p c (b j) -> p c b j", b=SB)
        uext_s = uext[:, :, UP:UEXT].rearrange("p c (j b) -> p c b j", b=SB)

        dw_cols = vec[:, V_DW:V_DW + KC * TAPS].rearrange("p (k c) -> p k c", c=KC)

        norms = [
            (lambda c: zT[:, c, :], NT, V_MG, V_MB),
            (lambda c: zT[:, c, :], NT, V_FG, V_FB),
            (lambda c: cacc[:, c, :], NM, V_CG, V_CB),
            (lambda c: zT[:, c, META:NT], NM, V_MG + KC, V_MB + KC),
        ]

        IN_JOBS = [(i, half) for i in range(3) for half in range(2)] + [("pool", 0), ("pool", 1)]
        VEC_BANK = 7
        N_IN = len(IN_JOBS) + 1
        CONV_JOBS = [(i, half) for i in range(2) for half in range(2)]
        U_JOBS = [(part, half) for part in range(2) for half in range(2)]
        X_JOBS = [(i, half) for i in range(3) for half in range(2)]
        T_CONVJ = N_IN
        T_UJ = T_CONVJ + len(CONV_JOBS)
        T_XJ = T_UJ + len(U_JOBS)
        A_IN = 5
        A_CONV = A_IN + len(CONV_JOBS)
        A_U = A_CONV + len(U_JOBS)
        RTOT = E + 1
        SCAT = 6 * (E + 1)
        SCATTER_BANKS = (1, 4, 5, 3, 6, 7)
        MEAN_LAG = 2
        KEEP_BUSY = 12
        MEAN_AHEAD = 4
        U_BANKS = (6, 7, 0, 1)
        Z_BEFORE = (0, KC, 2 * KC, 2 * KC + 1)
        DIAGS = [(q, k0, min(k0 + 16, TAPS)) for q in range(Q0, KC) for k0 in (0, 16)]

        ACT_DIAGS = (5, 7)

        def diag_slot(j):
            return (T_W2 + j) % SPLIT

        block = ctx.enter_context(nc.Block())

        @block.sync
        def _(sp):
            def load(t, src, dst):
                if t >= RAW:
                    sp.wait_ge(split_ready, t - RAW + 1)
                elif t == FIRST_BORROWED:
                    sp.wait_ge(z_done, KC)
                sp.dma_start(dst(raw[t % RAW]), src).then_inc(raw_landed[t % RAW], 16)

            def load_vectors():
                rows = [(pool_scale[0:1], 1), (conv_b1[0:1], 2), (conv_dw_b[0:1], 1), (conv_ln_g[0:1], 1),
                        (conv_ln_b[0:1], 1), (conv_b2[0:1], 1), (ln_mix_g, 2), (ln_mix_b, 2),
                        (ln_ffn_g[0:1], 1), (ln_ffn_b[0:1], 1)]
                r0 = 0
                for src, k in rows:
                    sp.dma_start(vrows[r0:r0 + KC * k, 0, :],
                                  src.rearrange("a (c p) -> (a c) p", p=P)).then_inc(vec_landed, 16)
                    r0 += KC * k
                dw_rows = conv_dw[0].rearrange("k (c p) -> (k c) p", p=P)
                for i in range(2):
                    sp.dma_start(vrows[0:124, 1 + i, :], dw_rows[124 * i:124 * i + 124, :]).then_inc(vec_landed, 16)
                sp.dma_start(router[:], moe_router[0].rearrange("(c p) e -> p c e", p=P)).then_inc(router_landed, 16)

            sp.dma_start(xin[META:P, 0, :], x_prompt[0, 0:P - META, :]).then_inc(x_landed[0], 16)
            sp.dma_start(xin[:, 1, :], x_prompt[0, P - META:2 * P - META, :]).then_inc(x_landed[1], 16)
            sp.dma_start(xin[META:META + NS, 2, :], x_sample.rearrange("b t d -> (b t) d")).then_inc(x_landed[2], 16)
            sp.dma_start(poolw[:], pool_w[0].rearrange("g (c p) e -> p g c e", p=P)).then_inc(poolw_landed, 16)
            for i in range(NJ):
                for k, w in ((0, ffn_w_gate), (1, ffn_w_up)):
                    load(2 * i + k, w[0, :, i * TW:(i + 1) * TW].rearrange("(c p) f -> p c f", p=P), wide)
                if i == 0:
                    load_vectors()
            for i in range(NJ):
                load(T_DOWN + i, ffn_w_down[0, i * TW:(i + 1) * TW, :].rearrange("(c p) f -> p c f", p=P), tall)
            for i in range(NW1 // 2):
                for k in range(2):
                    lo = k * D + i * TW
                    load(T_W1 + 2 * i + k, conv_w1[0, :, lo:lo + TW].rearrange("(c p) f -> p c f", p=P), wide)
            sp.wait_ge(jlo_done, NJ)
            for i in range(2):
                sp.dma_start(sconv[0:4 * CCTX, i, :],
                             state_conv[0, 4 * i:4 * i + 4].rearrange("b j d -> (b j) d")).then_inc(sconv_landed, 16)
            for i in range(NW2):
                load(T_W2 + i, conv_w2[0, :, i * TW:(i + 1) * TW].rearrange("(c p) f -> p c f", p=P), wide)

            def expert_tile(e, j):
                if j < 2:
                    kind, i = j, 0
                elif j == TE - 1:
                    kind, i = 2, NJ - 1
                else:
                    kind, i = (j + 1) % 3, (j + 1) // 3
                    i -= kind == 2
                if kind == 2:
                    src = moe_w_down[0].rearrange("e (j r) f -> (e j) r f", r=TW)[bass.ds(e * NJ + i, 1)]
                    return src.rearrange("o (c p) f -> p (o c) f", p=P), tall
                w = (moe_w_gate, moe_w_up)[kind]
                return w[0, bass.ds(e, 1), :, i * TW:(i + 1) * TW].rearrange("o (c p) f -> p (o c) f", p=P), wide

            def load_expert(n, e, j):
                t = T_MOE + j
                sp.wait_ge(split_ready, n * TE + (t - RAW + 1))
                src, dst = expert_tile(e, j) if j < TE else expert_tile((e + 1) % E, j - TE)
                sp.dma_start(dst(raw[t % RAW]), src).then_inc(raw_landed[t % RAW], 16)

            for j in range(2):
                load_expert(0, 0, j)
            sp.dma_start(new_pool_prompt[0, 0], x_prompt[0, SEQ - PCTX:SEQ, :]).then_inc(stored, 16)
            sp.dma_start(new_pool_sample[0, :, 0:PCTX - ST_, :], state_pool[0, :, ST_:PCTX, :]).then_inc(stored, 16)
            sp.dma_start(new_pool_sample[0, :, PCTX - ST_:PCTX, :], x_sample).then_inc(stored, 16)
            sp.dma_start(new_conv_sample[0, :, 0:CCTX - ST_, :], state_conv[0, :, ST_:CCTX, :]).then_inc(stored, 16)
            sp.wait_ge(evac_a, A_U)
            sp.dma_start(new_conv_prompt[0, 0], unat[0:CCTX, 0, :]).then_inc(u_stored, 16)
            for t in range(ST_):
                sp.dma_start(new_conv_sample[0, :, CCTX - ST_ + t, :],
                             unat[t * SB:(t + 1) * SB, 1, :]).then_inc(u_stored, 16)

            def one_pass(r):
                with sp.Fori(0, E) as e:
                    for j in range(2, TE + 2):
                        load_expert(r * E + e, e, j)

            one_pass(0)
            sp.wait_ge(acc_ready, 6)
            sp.dma_start(g_row[:], ln_ffn_g[1, :].partition_broadcast(P)).then_inc(rows_landed, 16)
            sp.dma_start(b_row[:], ln_ffn_b[1, :].partition_broadcast(P)).then_inc(rows_landed, 16)
            sp.wait_ge(flag_ready, 1)
            largest = sp.value_load(most_i[0:1, 0:1], min_val=0, max_val=NM)
            with sp.If(largest > P):
                with sp.Fori(1, 3) as r:
                    one_pass(r)
                for j in range(2):
                    t = T_MOE + 3 * E * TE + j
                    sp.wait_ge(raw_landed[t % RAW], 16 * (t // RAW + 1))
            for j in range(2):
                t = T_MOE + E * TE + j
                sp.wait_ge(raw_landed[t % RAW], 16 * (t // RAW + 1))
            for i in range(3):
                sp.wait_ge(fin_out, i + 1)
                if i < 2:
                    sp.dma_start(y_prompt[0, i * P:(i + 1) * P, :], acc[:, i, :]).then_inc(stored, 16)
                else:
                    sp.dma_start(y_sample.rearrange("b t d -> (b t) d"), acc[0:NS, i, :]).then_inc(stored, 16)
            sp.wait_ge(u_stored, 16 * (1 + ST_))
            sp.wait_ge(stored, 16 * (4 + 3))

        @block.gpsimd
        def _(pool):
            pool.memset(ident[:], 0.0).then_inc(pool_step, 1)
            pool.wait_ge(pool_step, 1)
            pool.affine_select(out=ident[:], in_=ident[:], compare_op=ALU.not_equal, fill=1.0, base=0,
                               pattern=[[-1, P]], channel_multiplier=1).then_inc(consts_ready, 1)
            pool.memset(mean_mat[:], 1.0 / D).then_inc(consts_ready, 1)
            pool.memset(pext[:, :, 0:PCTX], 0.0).then_inc(ctx_zeroed, 1)
            pool.memset(eps[:], LN_EPS).then_inc(consts_ready, 1)
            pool.iota(slot_no[:], pattern=[[1, P]], base=0, channel_multiplier=0,
                      allow_small_or_imprecise_dtypes=True).then_inc(consts_ready, 1)
            pool.memset(ones[:], 1.0).then_inc(consts_ready, 1)
            pool.memset(before[:], 1.0).then_inc(pool_step, 1)
            pool.wait_ge(pool_step, 2)
            pool.affine_select(out=before[:], in_=before[:], compare_op=ALU.is_ge, fill=0.0, base=-1,
                               pattern=[[1, P]], channel_multiplier=-1).then_inc(consts_ready, 1)
            for t in (logits, gate, taken, slot_of):
                pool.memset(t[:], 0.0 if t is not slot_of else NEG).then_inc(consts_ready, 1)
            pool.wait_ge(var_done, 2)
            pool.memset(uext[:, :, 0:CCTX], 0.0).then_inc(ctx_zeroed, 1)
            pool.wait_ge(dw_lo_ready, 1)
            plan = ["d0", "d1", "d2", "p0", "d3", "p1", "p2", "d4", "p3", "p4", "d6", "p5", "p6", "p7"]
            for step in plan:
                j = int(step[1])
                if step[0] == "d":
                    q, k0, k1 = DIAGS[j]
                    if j < SPLIT:
                        pool.wait_ge(tile_used, T_W2 + j - SPLIT + 1)
                    else:
                        pool.wait_ge(diag_used, j - SPLIT + 1)
                    out = w_lo[diag_slot(j)][:, 0:(k1 - k0) * P].rearrange("p (k m) -> p k m", m=P)
                    pool.tensor_tensor(out, ident[:].unsqueeze(1).to_broadcast([P, k1 - k0, P]),
                                       dw_lo[:, k0:k1, q - Q0:q - Q0 + 1].to_broadcast([P, k1 - k0, P]),
                                       ALU.mult).then_inc(diag_lo_done, 1)
                else:
                    if j == 0:
                        pool.wait_ge(u_done, KC)
                        pool.wait_ge(tile_used, T_W2)
                    if j >= 2:
                        pool.wait_ge(prod_used, j - 1)
                    first = uext[:, j, UP:UP + 1]
                    windows = bass.AP(tensor=first.tensor, offset=first.offset,
                                      ap=[first.ap[0], [1, SB], [SB, ST_], [SB, TAPS]])
                    taps = dw_cols[:, :, j].unsqueeze(1).unsqueeze(1).to_broadcast([P, SB, ST_, TAPS])
                    pool.tensor_tensor(prod[:, j % 2].rearrange("p (b t) k -> p b t k", b=SB), windows, taps,
                                       ALU.mult).then_inc(prod_done, 1)
            pool.wait_ge(var_done, 4)
            pool.memset(xn_hi[:, 2, :].bitcast(F32), 0.0).then_inc(ctx_zeroed, 1)
            pool.memset(xn_lo[:, 2, :].bitcast(F32), 0.0).then_inc(ctx_zeroed, 1)
        N_CONSTS = 10

        @block.scalar
        def _(act):
            act.dma_start(xin[0:META, 0, :], meta).then_inc(x_landed[0], 16)
            act.dma_start(xin[0:META, 2, :], x_prompt[0, 2 * P - META:SEQ, :]).then_inc(x_landed[2], 16)
            act.dma_start(spool[0:SB * PCTX, :], state_pool[0].rearrange("b j d -> (b j) d")).then_inc(spool_landed, 16)
            def hi(t, n=None):
                if n is None:
                    act.wait_ge(raw_landed[t % RAW], 16 * (t // RAW + 1))
                    if t >= SPLIT:
                        act.wait_ge(tile_used, t - SPLIT + 1)
                else:
                    act.wait_ge(raw_landed[t % RAW], n * (16 * TE // RAW) + 16 * (t // RAW + 1))
                    act.wait_ge(tile_used, n * TE + (t - SPLIT + 1))
                act.copy(w_hi[t % SPLIT][:], raw[t % RAW][:]).then_inc(hi_ready, 1)

            n_evac = 0
            for job, (i, half) in enumerate(IN_JOBS):
                c0 = half * 4
                src = ps[job % 8][:, :].rearrange("p (c n) -> p c n", c=4)
                if i == "pool":
                    act.wait_ge(turned, job + 1)
                    for c in range(4):
                        last = act.copy(pext_s[:, c0 + c, :, 0:PCTX],
                                        src[:, c, 0:SB * PCTX].rearrange("p (b j) -> p b j", b=SB))
                    last.then_inc(evac_a, 1)
                elif half == 1 and i in (0, 1):
                    act.wait_ge(turned, job + 1)
                    act.copy(pext[:, c0:c0 + 4, PCTX + P * i:PCTX + P * (i + 1)], src).then_inc(evac_a, 1)
                elif half == 1 and i == 2:
                    act.wait_ge(turned, job + 1)
                    act.copy(pext[:, c0:c0 + 4, PCTX + 2 * P:PCTX + NPR], src[:, :, 0:META])
                    for c in range(4):
                        last = act.copy(pext_s[:, c0 + c, :, PCTX:PCTX + ST_],
                                        src[:, c, META:META + NS].rearrange("p (b j) -> p b j", b=SB))
                    last.then_inc(evac_a, 1)
            act.wait_ge(evac_a, A_IN)
            act.wait_ge(evac_v, 3)
            act.mul(zT[:, :, 0:NPR], pext[:, :, PCTX:PCTX + NPR], ALPHA)
            for c in range(KC):
                last = act.mul(zT[:, c, NPR:NT].rearrange("p (b j) -> p b j", b=SB),
                               pext_s[:, c, :, PCTX:PCTX + ST_], ALPHA)
            last.then_inc(resid_ready, 1)
            hi(0)
            hi(1)

            def preload(func):
                act.activation(std3[:, 0:1], eps[:, 0:1], func)

            def norm(L, following, tile=None):
                z, n, g, b = norms[L]
                preload(ACT.Sqrt)
                for c in range(KC):
                    act.wait_ge(xc_done, KC * L + c + 1)
                    act.activation(sq[:, c, 0:n], z(c), ACT.Square).then_inc(sq_done, 1)
                if tile is not None:
                    hi(tile)
                act.wait_ge(var_done, L + 1)
                act.activation(rs[:, 0:n], ps[1][:, 0:n], ACT.Sqrt, bias=eps[:, 0:1]).then_inc(std_done, 1)
                preload(following)

            def split_x(L):
                z, n, g, b = norms[L]
                for c in range(KC):
                    act.wait_ge(yg_done, KC * L + c + 1)
                    if L == 2:
                        act.activation(z(c), z(c), ACT.Silu, bias=v(b + c)).then_inc(y_done, 1)
                        act.wait_ge(y_done, c + 1)
                        act.copy(x_hi[:, c, 0:n], z(c)).then_inc(xhi_done, 1)
                    else:
                        act.activation(x_hi[:, c, 0:n], z(c), ACT.Identity, bias=v(b + c)).then_inc(xhi_done, 1)

            def scale_residual(L):
                for c in range(KC):
                    act.wait_ge(xlo_done, KC * L + c + 1)
                    act.activation(zT[:, c, :], zT[:, c, :], ACT.Identity, scale=ALPHA,
                                   bias=v((V_SCALE, V_B2)[L] + c)).then_inc(scaled, 1)

            norm(0, ACT.Silu)
            split_x(0)
            act.wait_ge(gains_ready, 1)
            scale_residual(0)
            for i in range(NJ):
                hi(2 * i + 2)
                hi(2 * i + 3)
                act.wait_ge(tile_used, 2 * i + 1)
                for s in range(2):
                    q = 2 * i + s
                    if q >= 2:
                        act.wait_ge(h_done, q - 1)
                    act.activation(sg[s][:], ps[2 * (q % 4)][:, 0:NT], ACT.Silu).then_inc(silu_done, 1)
            for i in range(-1, NJ):
                if i >= 0:
                    hi(T_DOWN + i + 2)
                if i + 1 < NJ:
                    act.wait_ge(h_done, 2 * (i + 2))
                    if i >= 1:
                        act.wait_ge(tile_used, T_DOWN + i)
                    act.copy(h_hi[(i + 1) % 2][:], h[:, 2 * i + 2:2 * i + 4, :]).then_inc(jhi_done, 1)
            norm(1, ACT.Sigmoid)
            for k, (i, half) in enumerate(CONV_JOBS):
                act.wait_ge(turned, T_CONVJ + k + 1)
                src = ps[2 + k][:, :].rearrange("p (c n) -> p c n", c=4)
                for c in range(4):
                    last = act.copy(uext_s[:, 4 * half + c, 4 * i:4 * i + 4, 0:CCTX],
                                    src[:, c, 0:4 * CCTX].rearrange("p (b j) -> p b j", b=4))
                last.then_inc(evac_a, 1)
            split_x(1)
            scale_residual(1)
            def diag_hi(j):
                q, k0, k1 = DIAGS[j]
                if j < SPLIT:
                    act.wait_ge(tile_used, T_W2 + j - SPLIT + 1)
                else:
                    act.wait_ge(diag_used, j - SPLIT + 1)
                for k in range(k0, k1):
                    last = act.mul(w_hi[diag_slot(j)][:, (k - k0) * P:(k - k0 + 1) * P], ident[:],
                                   v(V_DW + KC * k + q))
                if j in ACT_DIAGS:
                    for k in range(k0, k1):
                        last = act.mul(w_lo[diag_slot(j)][:, (k - k0) * P:(k - k0 + 1) * P], ident[:],
                                       dw_lo[:, k, q - Q0:q - Q0 + 1])
                last.then_inc(diag_hi_done, 1)

            for i in range(NW1 // 2):
                if i < NW1 // 2 - 1:
                    hi(T_W1 + 2 * i + 2)
                    hi(T_W1 + 2 * i + 3)
                else:
                    diag_hi(0)
                    diag_hi(1)
                act.wait_ge(tile_used, T_W1 + 2 * i + 2)
                for s in range(2):
                    q = 2 * i + s
                    if q >= 2:
                        act.wait_ge(u_done, q - 1)
                    act.activation(sg[s][:], ps[2 * (q % 4) + 1][:, 0:NT], ACT.Sigmoid,
                                   bias=v(V_B1 + KC + q)).then_inc(sig_done, 1)

            def uc_split(c):
                act.wait_ge(u_done, Q0 + c + 1)
                act.copy(uc_hi[:, c, :], uext[:, Q0 + c, META:META + UW]).then_inc(uc_hi_done, 1)

            def conv_evac(c):
                act.wait_ge(diag_used, 2 * c + 2)
                act.activation(cacc[:, Q0 + c, 0:SEQ], ps[2 + c][:, 0:SEQ], ACT.Identity,
                               bias=v(V_DWB + Q0 + c)).then_inc(conv_out, 1)

            uc_split(0)
            uc_split(1)
            diag_hi(2)
            uc_split(2)
            uc_split(3)
            diag_hi(3)
            for k, (part, half) in enumerate(U_JOBS):
                act.wait_ge(turned, T_UJ + k + 1)
                n = (CCTX, NS)[part]
                act.copy(unat[0:n, part, half * HALF:(half + 1) * HALF],
                         ps[U_BANKS[k]][0:n, :]).then_inc(evac_a, 1)
            for j in range(4, len(DIAGS)):
                diag_hi(j)
            for c in range(NPE):
                conv_evac(c)
            hi(T_W2)
            norm(2, ACT.Silu, T_W2 + 1)
            split_x(2)
            for i in range(NW2):
                hi(T_W2 + 2 + i)
            norm(3, ACT.Exp)
            for c in range(KC):
                act.wait_ge(yg_done, KC * 3 + c + 1)
                act.activation(norms[3][0](c), norms[3][0](c), ACT.Identity,
                               bias=v(norms[3][3] + c)).then_inc(y_done, 1)
            for k, (i, half) in enumerate(X_JOBS):
                n = OUT_ROWS[i]
                act.wait_ge(turned, T_XJ + k + 1)
                if i == 2:
                    act.wait_ge(ctx_zeroed, 4)
                cols = slice(half * HALF, (half + 1) * HALF)
                act.copy(xn_hi[0:n, i, cols], ps[(3 + k) % 8][0:n, :]).then_inc(xhi_done, 1)
            act.wait_ge(gap_ready, 1)
            act.activation(prob[:, :, 1:2], prob[:, :, 0:1], ACT.Exp).then_inc(exp_done, 1)
            preload(ACT.Silu)
            for k, (i, half) in enumerate(X_JOBS):
                n = OUT_ROWS[i]
                act.wait_ge(xlo_done, 3 * KC + k + 1)
                act.mul(acc[0:n, i, half * HALF:(half + 1) * HALF], ps[(3 + k) % 8][0:n, :],
                        ALPHA).then_inc(acc_ready, 1)
            act.wait_ge(u_stored, 16 * (1 + ST_))

            def xg_evac(g):
                for k in range(2):
                    act.wait_ge(gathered, 2 * g + (k + 1))
                    act.copy(xg_hi[:, 4 * k:4 * k + 4, :],
                             ps[1 + 2 * k][:, :].rearrange("p (c n) -> p c n", c=4)).then_inc(xg_hi_done, 1)

            def rows_evac(g):
                act.wait_ge(rows_gathered, g + 1)
                for k in range(2):
                    act.copy(xg_rows[:, k * HALF:(k + 1) * HALF], ps[1 + 2 * k][:, :]).then_inc(rows_out, 1)

            def one_pass(r):
                rows_evac(r * RTOT)
                xg_evac(r * RTOT)
                with act.Fori(0, E) as e:
                    n = r * E + e
                    t0 = n * TE

                    def silu(j, gate_tile):
                        act.wait_ge(tile_used, t0 + (T_MOE + gate_tile + 1))
                        act.wait_ge(h_done, n * NJ + (FC + j))
                        act.activation(sgn[:], ps[j % 2][:, 0:TW], ACT.Silu).then_inc(silu_done, 1)

                    def turn_evac(j):
                        act.wait_ge(h_turned, n * NJ + (j + 1))
                        act.copy(ht_hi[:], ps[4 + j % 2][:, 0:TR * P].rearrange("p (c n) -> p c n", c=TR))\
                            .then_inc(ht_hi_done, 1)

                    hi(T_MOE + 2, n)
                    hi(T_MOE + 3, n)
                    silu(0, 0)
                    for j in range(1, NJ):
                        g = 3 * j - 1
                        hi(T_MOE + g + 2, n)
                        turn_evac(j - 1)
                        if j == 1:
                            act.wait_ge(sel_turned, n + 1)
                            act.copy(sel_t[:], ps[5][:, 0:NM]).then_inc(sel_t_done, 1)
                        hi(T_MOE + g + 3, n)
                        silu(j, g)
                        hi(T_MOE + g + 4, n)
                    rows_evac(r * RTOT + e + 1)
                    turn_evac(NJ - 1)
                    xg_evac(r * RTOT + e + 1)
                    hi(T_MOE + TE + 1, n)
                    act.wait_ge(tile_used, t0 + (T_MOE + TE))
                    for k in range(2):
                        act.copy(yy_hi[:, k * HALF:(k + 1) * HALF], ps[6 + k][:, :]).then_inc(yy_hi_done, 1)

            one_pass(0)
            act.wait_ge(flag_ready, 1)
            largest = act.value_load(most_i[0:1, 0:1], min_val=0, max_val=NM)
            with act.If(largest > P):
                with act.Fori(1, 3) as r:
                    one_pass(r)
            for i in range(3):
                n = OUT_ROWS[i]
                act.wait_ge(fin_stats, i + 1)
                act.activation(std3[0:n, i:i + 1], mv[0:n, i, 1:2], ACT.Sqrt, bias=eps[0:n, 0:1]).then_inc(fin_std, 1)

        @block.tensor
        def _(pe):
            pe.wait_ge(consts_ready, N_CONSTS)
            for job, (i, half) in enumerate(IN_JOBS):
                c0 = half * 4
                dst = ps[job % 8][:, :].rearrange("p (c n) -> p c n", c=4)
                if i == "pool":
                    pe.wait_ge(spool_landed, 16)
                    n = SB * PCTX
                    for c in range(4):
                        last = pe.transpose(dst[:, c, 0:n], spool[0:n, (c0 + c) * P:(c0 + c + 1) * P], ident[0:n, 0:n])
                else:
                    pe.wait_ge(x_landed[i], 16 if i == 1 else 32)
                    n = IN_ROWS[i]
                    for c in range(4):
                        last = pe.transpose(dst[:, c, 0:n], xin[0:n, i, (c0 + c) * P:(c0 + c + 1) * P], ident[0:n, 0:n])
                last.then_inc(turned, 1)
            pe.wait_ge(poolw_landed, 16)
            pe.wait_ge(evac_a, A_IN)
            for g in range(4):
                if g == 3:
                    pe.wait_ge(vec_landed, 16 * 12)
                    pe.transpose(ps[VEC_BANK][:, 0:104], vrows[0:104, 0, :], ident[0:104, 0:104])
                    for k in range(2):
                        last = pe.transpose(ps[VEC_BANK][:, 104 + 124 * k:228 + 124 * k], vrows[0:124, 1 + k, :],
                                            ident[0:124, 0:124])
                    last.then_inc(turned, 1)
                    pe.wait_ge(evac_v, 4)
                pe.wait_ge(d_ready, g + 1)
                for e in range(2):
                    for c in range(2):
                        last = pe.matmul(ps[2 * g + e][:, 0:NT], poolw[:, g, c, e * P:(e + 1) * P],
                                         dT[:, 2 * g + c, :], start=(c == 0), stop=(c == 1))
                    last.then_inc(pooled, 1)

            def mean_part(L, chunks):
                z, n, g, b = norms[L]
                for c in chunks:
                    if L != 2:
                        pe.wait_ge(z_done, Z_BEFORE[L] + c + 1)
                    elif c == 0:
                        pe.wait_ge(z_done, Z_BEFORE[L] + 1)
                    elif c >= Q0:
                        pe.wait_ge(conv_out, c - Q0 + 1)
                    last = pe.matmul(ps[0][:, 0:n], mean_mat[:], z(c), start=(c == 0), stop=(c == KC - 1))
                    if c == KC - 1:
                        last.then_inc(mean_done, 1)

            def norm(L):
                z, n, g, b = norms[L]
                mean_part(L, range((0, KC - MEAN_LAG, 0, MEAN_AHEAD)[L], KC))
                if L == 1 or L == 3:
                    pe.wait_ge(z_done, Z_BEFORE[L] + 2)
                for c in range(KC):
                    pe.wait_ge(sq_done, KC * L + c + 1)
                    last = pe.matmul(ps[1][:, 0:n], mean_mat[:], sq[:, c, 0:n], start=(c == 0), stop=(c == KC - 1))
                last.then_inc(var_done, 1)
                for _ in range(KEEP_BUSY):
                    pe.matmul(ps[7][:, 0:P], mean_mat[:], mean_mat[:], start=True, stop=True)

            def feature_block(banks, n, t, blocks, x_base=None):
                wh, wl = wide(w_hi[t % SPLIT]), wide(w_lo[t % SPLIT])
                for c in range(KC):
                    if x_base is not None:
                        pe.wait_ge(xlo_done, x_base + c + 1)
                    for bank, s in zip(banks, blocks):
                        cols = slice(s * P, (s + 1) * P)
                        for k, (w, x) in enumerate(((wh, x_hi), (wh, x_lo), (wl, x_hi))):
                            last = pe.matmul(bank[:, 0:n], w[:, c, cols], x[:, c, 0:n],
                                             start=(c == 0 and k == 0), stop=(c == KC - 1 and k == 2))
                return last

            norm(0)
            for i in range(NJ):
                for kind in range(2):
                    t = 2 * i + kind
                    pe.wait_ge(split_ready, t + 1)
                    if t == 0:
                        last = feature_block((ps[0], ps[2]), NT, t, (0, 1), x_base=0)
                    for s in range(2 if t else 0):
                        q = 2 * i + s
                        if q >= 4:
                            pe.wait_ge(h_done, q - 3)
                        last = feature_block((ps[2 * (q % 4) + kind],), NT, t, (s,))
                    last.then_inc(tile_used, 1)
            pe.wait_ge(h_done, FC)
            for i in range(NJ):
                t = T_DOWN + i
                pe.wait_ge(split_ready, t + 1)
                pe.wait_ge(jlo_done, i + 1)
                wh, wl = tall(w_hi[t % SPLIT]), tall(w_lo[t % SPLIT])
                for s in range(TR):
                    for c in range(KC):
                        cols = slice(c * P, (c + 1) * P)
                        for k, (w, x) in enumerate(((wh, h_hi), (wh, h_lo), (wl, h_hi))):
                            last = pe.matmul(ps[c][:, 0:NT], w[:, s, cols], x[i % 2][:, s, :],
                                             start=(i == 0 and s == 0 and k == 0),
                                             stop=(i == NJ - 1 and s == TR - 1 and k == 2))
                        if i == NJ - 1 and s == TR - 1:
                            if c < KC - 1:
                                last.then_inc(down_done, 1)
                            else:
                                last.then_inc(tile_used, 1)
                            if c >= MEAN_LAG:
                                mean_part(1, [c - MEAN_LAG])
                if i < NJ - 1:
                    last.then_inc(tile_used, 1)
            norm(1)
            pe.wait_ge(sconv_landed, 32)
            pe.wait_ge(z_done, 2 * KC)
            for k, (i, half) in enumerate(CONV_JOBS):
                n = 4 * CCTX
                for c in range(4):
                    f = 4 * half + c
                    last = pe.transpose(ps[2 + k][:, c * P:c * P + n], sconv[0:n, i, f * P:(f + 1) * P], ident[0:n, 0:n])
                last.then_inc(turned, 1)
            pe.wait_ge(evac_a, A_CONV)
            for i in range(NW1 // 2):
                for kind in range(2):
                    t = T_W1 + 2 * i + kind
                    pe.wait_ge(split_ready, t + 1)
                    if t == T_W1:
                        last = feature_block((ps[0], ps[2]), NT, t, (0, 1), x_base=KC)
                    for s in range(2 if t > T_W1 else 0):
                        q = 2 * i + s
                        if q >= 4:
                            pe.wait_ge(u_done, q - 3)
                        last = feature_block((ps[2 * (q % 4) + kind],), NT, t, (s,))
                    last.then_inc(tile_used, 1)
            pe.wait_ge(u_done, KC)
            for k, (part, half) in enumerate(U_JOBS):
                dst = ps[U_BANKS[k]]
                for c in range(4):
                    f = 4 * half + c
                    src = uext[:, f, UP - CCTX:UP] if part == 0 else uext[:, f, UP + CCTX * SB:UEXT]
                    n = (CCTX, NS)[part]
                    last = pe.transpose(dst[0:n, c * P:(c + 1) * P], src, ident[:])
                last.then_inc(turned, 1)
            for j, (q, k0, k1) in enumerate(DIAGS):
                c = q - Q0
                pe.wait_ge(uc_lo_done, c + 1)
                pe.wait_ge(diag_hi_done, j + 1)
                pe.wait_ge(diag_lo_done, j + 1 - sum(a <= j for a in ACT_DIAGS))
                for k in range(k0, k1):
                    cols = slice((k - k0) * P, (k - k0 + 1) * P)
                    for m, (w, x) in enumerate(((w_hi, uc_hi), (w_hi, uc_lo), (w_lo, uc_hi))):
                        last = pe.matmul(ps[2 + c][:, 0:SEQ], w[diag_slot(j)][:, cols], x[:, c, k:k + SEQ],
                                         start=(k == 0 and m == 0), stop=(k == TAPS - 1 and m == 2))
                last.then_inc(diag_used, 1)
            pe.wait_ge(evac_a, A_U)
            norm(2)
            for i in range(NW2):
                t = T_W2 + i
                pe.wait_ge(split_ready, t + 1)
                if i == NW2 - 1:
                    mean_part(3, range(MEAN_AHEAD))
                last = feature_block((ps[2 * i], ps[2 * i + 1]), NM, t, (0, 1), 2 * KC if i == 0 else None)
                last.then_inc(tile_used, 1)
            norm(3)
            pe.wait_ge(router_landed, 16)
            pe.wait_ge(z_done, Z_BEFORE[3] + KC)
            for c in range(KC):
                pe.wait_ge(y_done, KC + c + 1)
                for i in range(3):
                    n = OUT_ROWS[i]
                    last = pe.matmul(ps[i][0:n, 0:E], zT[:, c, META + P * i:META + P * i + n],
                                     router[:, c, :], start=(c == 0), stop=(c == KC - 1))
            last.then_inc(routed, 1)
            for k, (i, half) in enumerate(X_JOBS):
                if k == 5:
                    pe.wait_ge(gap_ready, 1)
                n = OUT_ROWS[i]
                for c in range(4):
                    f = 4 * half + c
                    last = pe.transpose(ps[(3 + k) % 8][0:n, c * P:(c + 1) * P],
                                        zT[:, f, META + P * i:META + P * i + n], ident[:])
                last.then_inc(turned, 1)
            pe.wait_ge(mask_ready, 1)
            for i in range(3):
                for k in range(i + 1):
                    n = OUT_ROWS[k]
                    last = pe.matmul(ps[1][:, i * E:(i + 1) * E], (before if k == i else ones)[0:n, :], taken[0:n, k, :],
                              start=(k == 0), stop=(k == i))
            last.then_inc(placed, 1)
            for k in range(3):
                n = OUT_ROWS[k]
                last = pe.matmul(ps[2][:, 0:E], ones[0:n, :], taken[0:n, k, :], start=(k == 0), stop=(k == 2))
            last.then_inc(counted, 1)

            def gather_rows(g):
                pe.wait_ge(sel_ready, g + 1)
                for i in range(3):
                    for m, x in enumerate((xn_hi, xn_lo)):
                        for half in range(2):
                            last = pe.matmul(ps[1 + 2 * half][:, :], sel[:, i, :],
                                             x[:, i, half * HALF:(half + 1) * HALF],
                                             start=(i == 0 and m == 0), stop=(i == 2 and m == 1))
                last.then_inc(rows_gathered, 1)

            def gather_turn(g):
                for half in range(2):
                    pe.wait_ge(rows_out, 2 * g + 2)
                    for c in range(4):
                        f = (4 * half + c) * P
                        last = pe.transpose(ps[1 + 2 * half][:, c * P:(c + 1) * P], xg_rows[:, f:f + P], ident[:])
                    last.then_inc(gathered, 1)

            def scatter(y_count):
                pe.wait_ge(yy_lo_done, y_count)
                for k in range(6):
                    i, half = k // 2, k % 2
                    n = OUT_ROWS[i]
                    for m, y in enumerate((yy_hi, yy_lo)):
                        last = pe.matmul(ps[SCATTER_BANKS[k]][0:n, :], sel_t[:, P * i:P * i + n],
                                         y[:, half * HALF:(half + 1) * HALF], start=(m == 0), stop=(m == 1))
                    last.then_inc(spread, 1)

            def one_pass(r):
                gather_rows(r * RTOT)
                gather_turn(r * RTOT)
                with pe.Fori(0, E) as e:
                    n = r * E + e
                    scattered = r * SCAT + e * 6

                    def rows_block(bank, j, t):
                        pe.wait_ge(split_ready, n * TE + (t + 1))
                        wh, wl = wide(w_hi[t % SPLIT]), wide(w_lo[t % SPLIT])
                        for c in range(KC):
                            for k, (x, w) in enumerate(((xg_hi, wh), (xg_hi, wl), (xg_lo, wh))):
                                last = pe.matmul(bank[:, 0:TW], x[:, c, :], w[:, c, :],
                                                 start=(c == 0 and k == 0), stop=(c == KC - 1 and k == 2))
                        last.then_inc(tile_used, 1)

                    def turn_h(j):
                        pe.wait_ge(h_done, n * NJ + (FC + j + 1))
                        if j >= 2:
                            pe.wait_ge(ht_lo_done, n * NJ + (j - 1))
                        for s in range(TR):
                            last = pe.transpose(ps[4 + j % 2][:, s * P:(s + 1) * P], hn[:, s * P:(s + 1) * P], ident[:])
                        last.then_inc(h_turned, 1)

                    def down(j, t):
                        pe.wait_ge(split_ready, n * TE + (t + 1))
                        pe.wait_ge(ht_lo_done, n * NJ + (j + 1))
                        wh, wl = tall(w_hi[t % SPLIT]), tall(w_lo[t % SPLIT])
                        for s in range(TR):
                            for half in range(2):
                                cols = slice(half * HALF, (half + 1) * HALF)
                                for k, (x, w) in enumerate(((ht_hi, wh), (ht_hi, wl), (ht_lo, wh))):
                                    last = pe.matmul(ps[6 + half][:, :], x[:, s, :], w[:, s, cols],
                                                     start=(j == 0 and s == 0 and k == 0),
                                                     stop=(j == NJ - 1 and s == TR - 1 and k == 2))
                        last.then_inc(tile_used, 1)

                    for j in range(NJ):
                        g = T_MOE + (3 * j - 1 if j else 0)
                        if j == 0:
                            pe.wait_ge(acc_ready, 6)
                            pe.wait_ge(xg_lo_done, (r * RTOT + e) * 2 + 2)
                        if j == 1:
                            pe.wait_ge(summed, scattered + 1)
                        pe.wait_ge(silu_done, n * NJ + (FC + max(0, j - 1)))
                        rows_block(ps[j % 2], j, g)
                        if j == 1:
                            pe.wait_ge(summed, scattered + 2)
                        if j >= 1:
                            turn_h(j - 1)
                        if j == 1:
                            pe.wait_ge(summed, scattered + 3)
                            for i in range(3):
                                m = OUT_ROWS[i]
                                last = pe.transpose(ps[5][:, P * i:P * i + m], sel[0:m, i, :].bitcast(F32),
                                                    ident[0:m, 0:m])
                            last.then_inc(sel_turned, 1)
                        if j == 2:
                            pe.wait_ge(sel_t_done, n + 1)
                        pe.wait_ge(h_done, n * NJ + (FC + max(0, j - 1)))
                        if j == 1:
                            pe.wait_ge(summed, scattered + 4)
                        rows_block(ps[2 + j % 2], j, g + 1)
                        if j == 1:
                            pe.wait_ge(summed, scattered + 6)
                        if j == 0:
                            pe.wait_ge(yy_cleared, r + 1)
                            scatter(n * 2 + 2)
                        else:
                            if j == NJ - 1:
                                gather_rows(r * RTOT + e + 1)
                            down(j - 1, g + 2)
                    turn_h(NJ - 1)
                    gather_turn(r * RTOT + e + 1)
                    down(NJ - 1, T_MOE + TE - 1)
                scatter((r * E + E) * 2 + 2)

            pe.wait_ge(acc_ready, 1)
            pe.wait_ge(xlo_done, 3 * KC + 6)
            one_pass(0)
            pe.wait_ge(flag_ready, 1)
            largest = pe.value_load(most_i[0:1, 0:1], min_val=0, max_val=NM)
            with pe.If(largest > P):
                with pe.Fori(1, 3) as r:
                    one_pass(r)

        @block.vector
        def _(dve):
            steps = [0]

            def link(ins):
                steps[0] += 1
                ins.then_inc(dve_step, 1)
                dve.wait_ge(dve_step, steps[0])

            def lo(t, n=None):
                dve.wait_ge(hi_ready, t + 1 if n is None else n * TE + (t + 1))
                dve.tensor_tensor(w_lo[t % SPLIT][:], raw[t % RAW][:], w_hi[t % SPLIT][:],
                                  ALU.subtract).then_inc(split_ready, 1)

            for job, (i, half) in enumerate(IN_JOBS):
                src = ps[job % 8][:, :].rearrange("p (c n) -> p c n", c=4)
                if half == 0 and i in (0, 1):
                    dve.wait_ge(turned, job + 1)
                    dve.tensor_copy(pext[:, 0:4, PCTX + P * i:PCTX + P * (i + 1)], src).then_inc(evac_v, 1)
                elif half == 0 and i == 2:
                    dve.wait_ge(turned, job + 1)
                    dve.tensor_copy(pext[:, 0:4, PCTX + 2 * P:PCTX + NPR], src[:, :, 0:META])
                    for c in range(4):
                        last = dve.tensor_copy(pext_s[:, c, :, PCTX:PCTX + ST_],
                                               src[:, c, META:META + NS].rearrange("p (b j) -> p b j", b=SB))
                    last.then_inc(evac_v, 1)
            dve.wait_ge(consts_ready, N_CONSTS)
            link(dve.tensor_scalar(recip[:], slot_no[:, 0:16], 1.0, None, ALU.add))
            link(dve.reciprocal(recip[:], recip[:]))

            def residual(chunks):
                for c in chunks:
                    dve.wait_ge(pooled, c + 1)
                    dve.scalar_tensor_tensor(out=zT[:, c, :], in0=ps[c][:, 0:NT], scalar=v(V_SCALE + c),
                                             in1=zT[:, c, :], op0=ALU.mult, op1=ALU.add).then_inc(z_done, 1)

            dve.wait_ge(evac_v, 3)
            dve.wait_ge(ctx_zeroed, 1)
            for g, w in enumerate(WINDOWS):
                dve.wait_ge(evac_a, A_IN - 1 if g < 2 else A_IN)
                if g == 3:
                    dve.wait_ge(turned, N_IN)
                    dve.tensor_copy(vec[:], ps[VEC_BANK][:, 0:104 + KC * TAPS]).then_inc(evac_v, 1)
                    dve.wait_ge(evac_v, 4)
                    dve.wait_ge(resid_ready, 1)
                    residual(range(4))
                x = pext[:, 2 * g:2 * g + 2, :]
                if g:
                    dve.wait_ge(d_ready, g)
                cur, other, have = win_a, win_b, 2
                link(dve.tensor_tensor(cur[:, :, 1:PEXT], x[:, :, 1:PEXT], x[:, :, 0:PEXT - 1], ALU.add))
                while have < w:
                    lo_col = 2 * have - 1
                    link(dve.tensor_tensor(other[:, :, lo_col:PEXT], cur[:, :, lo_col:PEXT],
                                           cur[:, :, lo_col - have:PEXT - have], ALU.add))
                    cur, other, have = other, cur, 2 * have
                out = dT[:, 2 * g:2 * g + 2, :]
                link(dve.scalar_tensor_tensor(out=out[:, :, 0:NPR], in0=cur[:, :, PCTX:PCTX + NPR], scalar=1.0 / w,
                                              in1=x[:, :, PCTX:PCTX + NPR], op0=ALU.mult, op1=ALU.subtract))
                for c in range(2):
                    link(dve.tensor_tensor(out[:, c, 0:w], cur[:, c, PCTX:PCTX + w], recip[:, 0:w], ALU.mult))
                    link(dve.tensor_tensor(out[:, c, 0:w], out[:, c, 0:w], x[:, c, PCTX:PCTX + w], ALU.subtract))
                    cur_s = cur[:, c, PCTX + NPR:PEXT].rearrange("p (b j) -> p b j", b=SB)[:, :, PCTX:PCTX + ST_]
                    last = dve.scalar_tensor_tensor(
                        out=out[:, c, NPR:NT].rearrange("p (b j) -> p b j", b=SB), in0=cur_s, scalar=1.0 / w,
                        in1=pext_s[:, 2 * g + c, :, PCTX:PCTX + ST_], op0=ALU.mult, op1=ALU.subtract)
                last.then_inc(d_ready, 1)
            residual((4, 5))
            lo(0)
            residual((6, 7))

            def norm(L):
                z, n, g, b = norms[L]
                if L == 2:
                    lo(T_W2)
                dve.wait_ge(mean_done, L + 1)
                dve.wait_ge(z_done, Z_BEFORE[L] + (KC if L != 2 else 1))
                if L == 2:
                    dve.wait_ge(conv_out, NPE)
                for c in range(KC):
                    dve.tensor_tensor(z(c), z(c), ps[0][:, 0:n], ALU.subtract).then_inc(xc_done, 1)
                if L < 2:
                    lo((1, T_W1 + 1)[L])
                dve.wait_ge(std_done, L + 1)
                dve.wait_ge(xc_done, KC * (L + 1))
                link(dve.reciprocal(rs[:, 0:n], rs[:, 0:n]))

                def low(c):
                    dve.wait_ge(xhi_done, KC * L + c + 1)
                    if L < 2:
                        dve.wait_ge(yg_done, KC * L + c + 1)
                        ins = dve.scalar_tensor_tensor(out=x_lo[:, c, 0:n], in0=z(c), scalar=v(b + c),
                                                       in1=x_hi[:, c, 0:n], op0=ALU.add, op1=ALU.subtract)
                    else:
                        ins = dve.tensor_tensor(x_lo[:, c, 0:n], z(c), x_hi[:, c, 0:n], ALU.subtract)
                    ins.then_inc(xlo_done, 1)

                for c in range(KC):
                    dve.scalar_tensor_tensor(out=z(c), in0=z(c), scalar=v(g + c), in1=rs[:, 0:n],
                                             op0=ALU.mult, op1=ALU.mult).then_inc(yg_done, 1)
                    if L < 3 and c >= 1:
                        low(c - 1)
                if L < 3:
                    low(KC - 1)

            dve.wait_ge(z_done, KC)
            dve.tensor_scalar(vec[:, V_SCALE:V_SCALE + KC], vec[:, V_MB:V_MB + KC], ALPHA, None, ALU.mult)
            dve.scalar_tensor_tensor(out=vec[:, V_B2:V_B2 + KC], in0=vec[:, V_FB:V_FB + KC], scalar=ALPHA,
                                     in1=vec[:, V_B2:V_B2 + KC], op0=ALU.mult, op1=ALU.add).then_inc(gains_ready, 1)
            norm(0)
            for i in range(NJ):
                lo(2 * i + 2)
                lo(2 * i + 3)
                dve.wait_ge(tile_used, 2 * i + 2)
                for s in range(2):
                    q = 2 * i + s
                    dve.wait_ge(silu_done, q + 1)
                    dve.tensor_tensor(h[:, q, :], sg[s][:], ps[2 * (q % 4) + 1][:, 0:NT], ALU.mult).then_inc(h_done, 1)
            for i in range(-1, NJ):
                if 0 <= i < NJ - 1:
                    lo(T_DOWN + i + 2)
                if i + 1 < NJ:
                    k = (i + 1) % 2
                    dve.wait_ge(jhi_done, i + 2)
                    if i < 0:
                        dve.wait_ge(h_done, FC)
                    dve.tensor_tensor(h_lo[k][:], h[:, 2 * i + 2:2 * i + 4, :], h_hi[k][:],
                                      ALU.subtract).then_inc(jlo_done, 1)
            for c in range(KC):
                if c < KC - 1:
                    dve.wait_ge(down_done, c + 1)
                else:
                    dve.wait_ge(tile_used, T_W1)
                dve.wait_ge(scaled, c + 1)
                dve.tensor_tensor(zT[:, c, :], zT[:, c, :], ps[c][:, 0:NT], ALU.add).then_inc(z_done, 1)
            norm(1)
            dve.wait_ge(ctx_zeroed, 2)
            dve.wait_ge(evac_a, A_CONV)
            dve.wait_ge(tile_used, T_W1)
            link(dve.tensor_copy(dw_hi[:], dw_cols[:, :, Q0:KC]))
            dve.tensor_tensor(dw_lo[:], dw_cols[:, :, Q0:KC], dw_hi[:], ALU.subtract).then_inc(dw_lo_ready, 1)
            dve.wait_ge(dw_lo_ready, 1)
            taps_done = [0] * KC
            convolved = []

            def convolve(pair, count):
                for _ in range(count):
                    for q in (2 * pair, 2 * pair + 1):
                        k = taps_done[q]
                        out, src = cacc[:, q, 0:SEQ], uext[:, q, META + k:META + k + SEQ]
                        if k == 0:
                            ins = dve.tensor_scalar(out, src, v(V_DW + q), v(V_DWB + q), ALU.mult, ALU.add)
                        else:
                            dve.wait_ge(conv_step, len(convolved) - convolved[::-1].index(q))
                            ins = dve.scalar_tensor_tensor(out=out, in0=src, scalar=v(V_DW + KC * k + q), in1=out,
                                                           op0=ALU.mult, op1=ALU.add)
                        ins.then_inc(conv_step, 1)
                        convolved.append(q)
                        taps_done[q] += 1

            for i in range(NW1 // 2):
                if i < NW1 // 2 - 1:
                    lo(T_W1 + 2 * i + 2)
                    if i:
                        convolve(0, 4)
                    lo(T_W1 + 2 * i + 3)
                if i:
                    convolve(0, 4)
                for s in range(2):
                    q = 2 * i + s
                    dve.wait_ge(sig_done, q + 1)
                    src = ps[2 * (q % 4)]
                    dve.scalar_tensor_tensor(out=uext[:, q, CCTX:UP], in0=src[:, 0:NPR], scalar=v(V_B1 + q),
                                             in1=sg[s][:, 0:NPR], op0=ALU.add, op1=ALU.mult)
                    dve.scalar_tensor_tensor(out=uext_s[:, q, :, CCTX:CCTX + ST_],
                                             in0=src[:, NPR:NT].rearrange("p (b j) -> p b j", b=SB), scalar=v(V_B1 + q),
                                             in1=sg[s][:, NPR:NT].rearrange("p (b j) -> p b j", b=SB),
                                             op0=ALU.add, op1=ALU.mult).then_inc(u_done, 1)
                dve.wait_ge(u_done, 2 * i + 2)
            for c in range(NPE):
                dve.wait_ge(uc_hi_done, c + 1)
                dve.tensor_tensor(uc_lo[:, c, :], uext[:, Q0 + c, META:META + UW], uc_hi[:, c, :],
                                  ALU.subtract).then_inc(uc_lo_done, 1)

            def sum_windows(c):
                dve.wait_ge(prod_done, c + 1)
                dve.tensor_reduce(cacc[:, c, SEQ:NM], prod[:, c % 2], AX.X, ALU.add).then_inc(prod_used, 1)

            convolve(0, TAPS - taps_done[0])
            for c in range(KC):
                convolve(1, min(4, TAPS - taps_done[2]))
                sum_windows(c)
            dve.wait_ge(prod_used, KC)
            dve.tensor_tensor(cacc[:, :, SEQ:NM], cacc[:, :, SEQ:NM],
                              vec[:, V_DWB:V_DWB + KC].unsqueeze(2).to_broadcast([P, KC, NS]), ALU.add).then_inc(z_done, 1)
            dve.wait_ge(conv_step, len(convolved))
            norm(2)
            lo(T_W2 + 1)
            for i in range(NW2):
                lo(T_W2 + 2 + i)
                dve.wait_ge(tile_used, T_W2 + i + 1)
                for s in range(2):
                    q = 2 * i + s
                    dve.wait_ge(scaled, KC + q + 1)
                    dve.tensor_tensor(zT[:, q, META:NT], zT[:, q, META:NT], ps[q][:, 0:NM], ALU.add).then_inc(z_done, 1)
            norm(3)
            dve.wait_ge(routed, 1)
            for i in range(3):
                n = OUT_ROWS[i]
                last = dve.tensor_copy(logits[0:n, i, :], ps[i][0:n, 0:E])
            link(last)
            for i in range(3):
                last = dve.max(top_v[:, i, :], logits[:, i, :])
            link(last)
            for i in range(3):
                last = dve.max_index(top_i[:, i, :], top_v[:, i, :], logits[:, i, :])
            link(last)
            dve.tensor_tensor(prob[:, :, 0:1], top_v[:, :, 1:2], top_v[:, :, 0:1], ALU.subtract).then_inc(gap_ready, 1)
            link(dve.tensor_copy(top_f[:], top_i[:, :, 0:2]))
            for i in range(3):
                for k, pick in enumerate((pick1, pick2)):
                    last = dve.tensor_scalar(pick[:, i, :], slot_no[:, 0:E], top_f[:, i, k:k + 1], None, ALU.is_equal)
            link(last)
            for i in range(3):
                n = OUT_ROWS[i]
                last = dve.tensor_tensor(taken[0:n, i, :], pick1[0:n, i, :], pick2[0:n, i, :], ALU.add)
            last.then_inc(mask_ready, 1)
            for k, (i, half) in enumerate(X_JOBS):
                n = OUT_ROWS[i]
                dve.wait_ge(xhi_done, 3 * KC + k + 1)
                if i == 2:
                    dve.wait_ge(ctx_zeroed, 4)
                cols = slice(half * HALF, (half + 1) * HALF)
                dve.tensor_tensor(xn_lo[0:n, i, cols], ps[(3 + k) % 8][0:n, :], xn_hi[0:n, i, cols],
                                  ALU.subtract).then_inc(xlo_done, 1)

            dve.wait_ge(placed, 1)
            dve.wait_ge(mask_ready, 1)
            for i in range(3):
                last = dve.scalar_tensor_tensor(out=slot_of[:, i, 0:E], in0=ps[1][:, i * E:(i + 1) * E], scalar=1.0,
                                                in1=taken[:, i, :], op0=ALU.add, op1=ALU.mult)
            link(last)
            link(dve.tensor_scalar(slot_of[:, :, 0:E], slot_of[:, :, 0:E], 1.0, None, ALU.subtract))
            def select(e):
                for i in range(3):
                    last = dve.tensor_scalar(sel[:, i, :], slot_no[:], slot_of[:, i, bass.ds(e, 1)], None, ALU.is_equal)
                last.then_inc(sel_ready, 1)

            dve.wait_ge(turned, T_XJ + len(X_JOBS))
            select(0)
            dve.wait_ge(exp_done, 1)
            link(dve.tensor_scalar(prob[:, :, 2:3], prob[:, :, 1:2], 1.0, None, ALU.add))
            link(dve.reciprocal(prob[:, :, 2:3], prob[:, :, 2:3]))
            link(dve.tensor_tensor(prob[:, :, 3:4], prob[:, :, 1:2], prob[:, :, 2:3], ALU.mult))
            for i in range(3):
                last = dve.tensor_scalar(pick1[:, i, :], pick1[:, i, :], prob[:, i, 2:3], None, ALU.mult)
            link(last)
            for i in range(3):
                n = OUT_ROWS[i]
                last = dve.scalar_tensor_tensor(out=gate[0:n, i, 1:1 + E], in0=pick2[0:n, i, :],
                                                scalar=prob[0:n, i, 3:4], in1=pick1[0:n, i, :],
                                                op0=ALU.mult, op1=ALU.add)
            link(last)
            dve.wait_ge(counted, 1)
            link(dve.tensor_reduce(most[:], ps[2][:, 0:E], AX.X, ALU.max))
            dve.tensor_copy(most_i[:], most[:]).then_inc(flag_ready, 1)

            def add_scattered(col, done, halves):
                for k in halves:
                    i, half = k // 2, k % 2
                    n = OUT_ROWS[i]
                    cols = slice(half * HALF, (half + 1) * HALF)
                    dve.wait_ge(spread, done + (k + 1))
                    dve.scalar_tensor_tensor(out=acc[0:n, i, cols], in0=ps[SCATTER_BANKS[k]][0:n, :],
                                             scalar=gate[0:n, i, bass.ds(col, 1)], in1=acc[0:n, i, cols],
                                             op0=ALU.mult, op1=ALU.add).then_inc(summed, 1)

            def xg_low(g):
                for k in range(2):
                    dve.wait_ge(xg_hi_done, 2 * g + (k + 1))
                    dve.tensor_tensor(xg_lo[:, 4 * k:4 * k + 4, :],
                                      ps[1 + 2 * k][:, :].rearrange("p (c n) -> p c n", c=4),
                                      xg_hi[:, 4 * k:4 * k + 4, :], ALU.subtract).then_inc(xg_lo_done, 1)

            def one_pass(r):
                with dve.Fori(0, E) as e:
                    n = r * E + e

                    def mult(j, up_tile):
                        dve.wait_ge(silu_done, n * NJ + (FC + j + 1))
                        dve.wait_ge(tile_used, n * TE + (T_MOE + up_tile + 1))
                        dve.tensor_tensor(hn[:], sgn[:], ps[2 + j % 2][:, 0:TW], ALU.mult).then_inc(h_done, 1)

                    def turn_low(j):
                        dve.wait_ge(ht_hi_done, n * NJ + (j + 1))
                        dve.tensor_tensor(ht_lo[:], ps[4 + j % 2][:, 0:TR * P].rearrange("p (c n) -> p c n", c=TR),
                                          ht_hi[:], ALU.subtract).then_inc(ht_lo_done, 1)

                    lo(T_MOE + 2, n)
                    lo(T_MOE + 3, n)
                    mult(0, 1)
                    dve.wait_ge(h_done, n * NJ + (FC + 1))
                    add_scattered(e, r * SCAT + e * 6, range(4))
                    for j in range(1, NJ):
                        g = 3 * j - 1
                        lo(T_MOE + g + 2, n)
                        if j == 1:
                            add_scattered(e, r * SCAT + e * 6, range(4, 6))
                        turn_low(j - 1)
                        lo(T_MOE + g + 3, n)
                        mult(j, g + 1)
                        lo(T_MOE + g + 4, n)
                        if j == 2:
                            dve.wait_ge(sel_turned, n + 1)
                            select(e + 1)
                    turn_low(NJ - 1)
                    xg_low(r * RTOT + e + 1)
                    lo(T_MOE + TE + 1, n)
                    for k in range(2):
                        dve.wait_ge(yy_hi_done, n * 2 + (k + 1))
                        cols = slice(k * HALF, (k + 1) * HALF)
                        dve.tensor_tensor(yy_lo[:, cols], ps[6 + k][:, :], yy_hi[:, cols],
                                          ALU.subtract).then_inc(yy_lo_done, 1)
                dve.wait_ge(yy_lo_done, (r * E + E) * 2 + 2)
                for i in range(3):
                    n = OUT_ROWS[i]
                    add_scattered(E, r * SCAT + 6 * E, (2 * i, 2 * i + 1))
                    dve.wait_ge(summed, r * SCAT + (6 * E + 2 * i + 2))
                    for k in range(2):
                        dve.bn_stats(stats[0:n, i, k, :], acc[0:n, i, k * HALF:(k + 1) * HALF]).then_inc(fin_half, 1)
                dve.wait_ge(fin_half, r * 6 + 6)

            dve.memset(sel_t[:].bitcast(F32), 0.0).then_inc(yy_lo_done, 1)
            dve.memset(yy_lo[:].bitcast(F32), 0.0).then_inc(yy_lo_done, 1)
            xg_low(0)
            dve.memset(yy_hi[:].bitcast(F32), 0.0).then_inc(yy_cleared, 1)
            dve.wait_ge(acc_ready, 6)
            one_pass(0)
            dve.wait_ge(flag_ready, 1)
            largest = dve.value_load(most_i[0:1, 0:1], min_val=0, max_val=NM)
            with dve.If(largest > P):
                with dve.Fori(1, 3) as r:
                    dve.wait_ge(gathered, r * (2 * RTOT))
                    dve.tensor_scalar(slot_of[:, :, 0:E], slot_of[:, :, 0:E], float(P), None,
                                      ALU.subtract).then_inc(slots_moved, 1)
                    dve.wait_ge(slots_moved, r)
                    select(0)
                    xg_low(r * RTOT)
                    dve.memset(yy_hi[:].bitcast(F32), 0.0).then_inc(yy_cleared, 1)
                    one_pass(r)
            for i in range(3):
                n = OUT_ROWS[i]
                dve.bn_aggr(mv[0:n, i, :], stats[0:n, i, :, :].rearrange("p a b -> p (a b)")).then_inc(fin_stats, 1)
            dve.wait_ge(rows_landed, 32)
            dve.wait_ge(fin_stats, 3)
            for i in range(3):
                n = OUT_ROWS[i]
                dve.scalar_tensor_tensor(out=acc[0:n, i, :], in0=acc[0:n, i, :], scalar=mv[0:n, i, 0:1],
                                         in1=g_row[0:n, :], op0=ALU.subtract, op1=ALU.mult).then_inc(fin_g, 1)
                dve.wait_ge(fin_std, i + 1)
                dve.reciprocal(std3[0:n, i:i + 1], std3[0:n, i:i + 1]).then_inc(fin_recip, 1)
                dve.wait_ge(fin_recip, i + 1)
                dve.scalar_tensor_tensor(out=acc[0:n, i, :], in0=acc[0:n, i, :], scalar=std3[0:n, i:i + 1],
                                         in1=b_row[0:n, :], op0=ALU.mult, op1=ALU.add).then_inc(fin_out, 1)



_INS = ['x_prompt', 'x_sample', 'state_pool', 'state_conv', 'meta', 'pool_w', 'pool_scale', 'conv_w1', 'conv_b1',
        'conv_dw', 'conv_dw_b', 'conv_ln_g', 'conv_ln_b', 'conv_w2', 'conv_b2', 'ln_mix_g', 'ln_mix_b', 'ln_ffn_g',
        'ln_ffn_b', 'ffn_w_gate', 'ffn_w_up', 'ffn_w_down', 'moe_router', 'moe_w_gate', 'moe_w_up', 'moe_w_down']
_OUTS = [((1, 256, 1024), 'float32'), ((8, 4, 1024), 'float32'), ((1, 1, 15, 1024), 'float32'),
         ((1, 1, 30, 1024), 'float32'), ((1, 8, 15, 1024), 'float32'), ((1, 8, 30, 1024), 'float32')]


def kernel(**inputs):
    import numpy as _np
    import concourse.bacc as _bacc
    from concourse import mybir as _mybir
    from concourse.bass_utils import run_bass_kernel_spmd as _run

    nc = _bacc.Bacc("TRN2", target_bir_lowering=False, num_devices=1)
    arrays, args = {}, []
    for name in _INS:
        a = _np.ascontiguousarray(inputs[name])
        arrays[f"in_{name}_dram"] = a
        args.append(nc.dram_tensor(f"in_{name}_dram", a.shape, _mybir.dt.from_np(a.dtype), kind="ExternalInput").ap())
    for i, (shape, dtype) in enumerate(_OUTS):
        dt = _mybir.dt.from_np(_np.dtype(dtype))
        args.append(nc.dram_tensor(f"out_{i}_dram", shape, dt, kind="ExternalOutput").ap())
    build_trunk(nc, *args)
    r = _run(nc, [arrays], core_ids=[0])
    return tuple(r.results[0][f"out_{i}_dram"] for i in range(len(_OUTS)))
```
